# Optimizing a Trainium2 kernel written in Bass

```python
import functools
import jax, jax.numpy as jnp
from jax import lax
import numpy as np

D_MODEL = 1024
BATCH = 1
SEQ = 512
DEPTH = 2
DEC_BATCH = 1
DEC_SEQ = 64
PAST_LEN = 256

CHUNK = 64
Q_BLOCK = 128
N_HEADS = 8
Q_LORA = 256
KV_LORA = 128
NOPE_DIM = 64
ROPE_DIM = 32
V_DIM = 64
QK_DIM = NOPE_DIM + ROPE_DIM
ATTN_W = N_HEADS * V_DIM
POOL_W = D_MODEL - ATTN_W
POOL_WINDOWS = (2, 4, 8, 16)
POOL_GROUPS = len(POOL_WINDOWS)
POOL_GC = POOL_W // POOL_GROUPS
POOL_HIST = max(POOL_WINDOWS) - 1
IN_W = Q_LORA + KV_LORA + ROPE_DIM + POOL_W
MIX_W = ATTN_W + POOL_W
D_FF = 128 * ((8 * D_MODEL // 3 + 127) // 128)
N_EXPERTS = 8
TOP_K = 2
D_EXPERT = D_FF // 2
N_DENSE = (DEPTH + 1) // 2
N_MOE = DEPTH // 2
ROPE_THETA = 10000.0
EPS = 1e-6
ATTN_SCALE = QK_DIM ** -0.5
NEG_INF = -1e30

kernel_name = 'hymba_mla_pool_stream_step'

def rms_norm(x, g):
    xf = x.astype(jnp.float32)
    y = xf * lax.rsqrt(jnp.mean(xf * xf, axis=-1, keepdims=True) + EPS)
    return (y * g.astype(jnp.float32)).astype(x.dtype)

def rope_tables(pos0, T):
    pos = jnp.arange(T, dtype=jnp.float32) + pos0
    inv = 1.0 / (ROPE_THETA ** (jnp.arange(0, ROPE_DIM, 2, dtype=jnp.float32) / ROPE_DIM))
    ang = pos[:, None] * inv[None, :]
    return jnp.cos(ang), jnp.sin(ang)

def apply_rope(x, cos, sin):
    extra = x.ndim - 3
    shp = (1, cos.shape[0]) + (1,) * extra + (cos.shape[1],)
    c = cos.reshape(shp)
    s = sin.reshape(shp)
    xf = x.astype(jnp.float32)
    half = ROPE_DIM // 2
    x1, x2 = xf[..., :half], xf[..., half:]
    return jnp.concatenate([x1 * c - x2 * s, x1 * s + x2 * c], axis=-1).astype(x.dtype)

def mla_queries(q_lat, p, cos, sin):
    B, T = q_lat.shape[:2]
    q = (rms_norm(q_lat, p['g_q_lat']) @ p['w_uq']).reshape(B, T, N_HEADS, QK_DIM)
    qn = rms_norm(q[..., :NOPE_DIM], p['g_qn_nope'])
    qr = apply_rope(rms_norm(q[..., NOPE_DIM:], p['g_qn_rope']), cos, sin)
    return qn, qr

def mla_cache_rows(kv_lat, kr_raw, p, cos, sin):
    ckv = rms_norm(kv_lat, p['g_kv_lat'])
    kr = apply_rope(rms_norm(kr_raw, p['g_kn_rope']), cos, sin)
    return ckv, kr

def mla_expand(ckv, p):
    B, S = ckv.shape[:2]
    kv = (ckv @ p['w_ukv']).reshape(B, S, N_HEADS, NOPE_DIM + V_DIM)
    kn = rms_norm(kv[..., :NOPE_DIM], p['g_kn_nope'])
    v = kv[..., NOPE_DIM:]
    return kn, v

def attend(qn, qr, kn, kr, v, mask):
    s = (jnp.einsum('bqhd,bkhd->bhqk', qn, kn).astype(jnp.float32)
         + jnp.einsum('bqhr,bkr->bhqk', qr, kr).astype(jnp.float32)) * ATTN_SCALE
    if mask is not None:
        s = jnp.where(mask[None, None], s, NEG_INF)
    prob = jax.nn.softmax(s, axis=-1).astype(v.dtype)
    return jnp.einsum('bhqk,bkhd->bqhd', prob, v)

def prompt_attention(qn, qr, kn, kr, v):
    B, T = qn.shape[:2]
    nb = T // Q_BLOCK
    qn_b = qn.reshape(B, nb, Q_BLOCK, N_HEADS, NOPE_DIM).transpose(1, 0, 2, 3, 4)
    qr_b = qr.reshape(B, nb, Q_BLOCK, N_HEADS, ROPE_DIM).transpose(1, 0, 2, 3, 4)
    key_chunk = jnp.arange(T) // CHUNK

    def block(args):
        qn_i, qr_i, i = args
        q_chunk = (i * Q_BLOCK + jnp.arange(Q_BLOCK)) // CHUNK
        mask = key_chunk[None, :] <= q_chunk[:, None]
        return attend(qn_i, qr_i, kn, kr, v, mask)

    out = lax.map(block, (qn_b, qr_b, jnp.arange(nb)))
    return out.transpose(1, 0, 2, 3, 4).reshape(B, T, ATTN_W)

def pool_mix(u, hist, pos0, w_pool, pool_scale):
    B, T = u.shape[:2]
    ext = jnp.concatenate([hist, u], axis=1)
    ef = ext.astype(jnp.float32)
    cs = jnp.concatenate([jnp.zeros((B, 1, POOL_W), jnp.float32), jnp.cumsum(ef, axis=1)], axis=1)
    pos = jnp.arange(T, dtype=jnp.float32) + pos0
    end = cs[:, POOL_HIST + 1:]
    parts = []
    for g, w in enumerate(POOL_WINDOWS):
        sl = slice(g * POOL_GC, (g + 1) * POOL_GC)
        start = POOL_HIST + 1 - w
        wsum = end[..., sl] - cs[:, start:start + T, sl]
        cnt = jnp.minimum(pos + 1.0, float(w))[None, :, None]
        parts.append(wsum / cnt - ef[:, POOL_HIST:, sl])
    d = jnp.concatenate(parts, axis=-1).astype(u.dtype).reshape(B, T, POOL_GROUPS, POOL_GC)
    y = jnp.einsum('btgc,gcd->btgd', d, w_pool).reshape(B, T, POOL_W) * pool_scale
    return y, ext[:, -POOL_HIST:]

def token_mixer(h, pos0, ckv_past, kr_past, pool_hist, p):
    B, T = h.shape[:2]
    z = h @ p['w_in']
    o1 = Q_LORA
    o2 = o1 + KV_LORA
    o3 = o2 + ROPE_DIM
    q_lat, kv_lat, kr_raw, u = z[..., :o1], z[..., o1:o2], z[..., o2:o3], z[..., o3:]
    cos, sin = rope_tables(pos0, T)
    qn, qr = mla_queries(q_lat, p, cos, sin)
    ckv_new, kr_new = mla_cache_rows(kv_lat, kr_raw, p, cos, sin)
    if ckv_past is None:
        kn, v = mla_expand(ckv_new, p)
        attn = prompt_attention(qn, qr, kn, kr_new, v)
        pool_hist = jnp.zeros((B, POOL_HIST, POOL_W), u.dtype)
    else:
        ckv_all = jnp.concatenate([ckv_past, ckv_new], axis=1)
        kr_all = jnp.concatenate([kr_past, kr_new], axis=1)
        kn, v = mla_expand(ckv_all, p)
        attn = attend(qn, qr, kn, kr_all, v, None).reshape(B, T, ATTN_W)
    pool_out, pool_new = pool_mix(u, pool_hist, pos0, p['w_pool'], p['pool_scale'])
    y = jnp.concatenate([attn, pool_out], axis=-1) @ p['w_out']
    return y, ckv_new, kr_new, pool_new

def swiglu(h, wg, wu, wd):
    return (jax.nn.silu(h @ wg) * (h @ wu)) @ wd

def moe_swiglu(h, w_router, b_router, wg, wu, wd):
    logits = (h @ w_router).astype(jnp.float32) + b_router.astype(jnp.float32)
    top_v, top_i = lax.top_k(logits, TOP_K)
    top_w = jax.nn.softmax(top_v, axis=-1)
    comb = jnp.sum(jax.nn.one_hot(top_i, N_EXPERTS, dtype=jnp.float32) * top_w[..., None],
                   axis=-2).astype(h.dtype)
    out = jnp.zeros_like(h)
    for e in range(N_EXPERTS):
        out = out + comb[..., e:e + 1] * swiglu(h, wg[e], wu[e], wd[e])
    return out

def trunk_layer(x, c, pos0, ckv_past, kr_past, pool_hist, p, ffn):
    mod = jax.nn.silu(c) @ p['w_ada'] + p['b_ada']
    sh1, sc1, g1, sh2, sc2, g2 = [m[:, None, :] for m in jnp.split(mod, 6, axis=-1)]
    h = rms_norm(x, p['g_mix']) * (1.0 + sc1) + sh1
    y, ckv_new, kr_new, pool_new = token_mixer(h, pos0, ckv_past, kr_past, pool_hist, p)
    x = x + g1 * y
    h = rms_norm(x, p['g_ffn']) * (1.0 + sc2) + sh2
    x = x + g2 * ffn(h)
    return x, ckv_new, kr_new, pool_new

def setup_inputs(seed: int = 0) -> dict:
    key = jax.random.key(seed)
    ks = jax.random.split(key, 31)
    f32 = jnp.float32
    D = D_MODEL

    def nrm(k, shape, scale=1.0):
        return jax.random.normal(k, shape, f32) * scale

    def gain(k, shape):
        return 1.0 + 0.05 * jax.random.normal(k, shape, f32)

    return {
        'x_prompt': nrm(ks[0], (BATCH, SEQ, D)),
        'x_sample': nrm(ks[1], (DEC_BATCH, DEC_SEQ, D)),
        'c_prompt': nrm(ks[2], (BATCH, D)),
        'c_sample': nrm(ks[3], (DEC_BATCH, D)),
        'cache_ckv': nrm(ks[4], (DEPTH, DEC_BATCH, PAST_LEN, KV_LORA)),
        'cache_krope': nrm(ks[5], (DEPTH, DEC_BATCH, PAST_LEN, ROPE_DIM)),
        'state_pool': nrm(ks[6], (DEPTH, DEC_BATCH, POOL_HIST, POOL_W)),
        'g_mix': gain(ks[7], (DEPTH, D)),
        'g_ffn': gain(ks[8], (DEPTH, D)),
        'w_ada': nrm(ks[9], (DEPTH, D, 6 * D), D ** -0.5),
        'b_ada': nrm(ks[10], (DEPTH, 6 * D), 0.02),
        'w_in': nrm(ks[11], (DEPTH, D, IN_W), D ** -0.5),
        'g_q_lat': gain(ks[12], (DEPTH, Q_LORA)),
        'g_kv_lat': gain(ks[13], (DEPTH, KV_LORA)),
        'w_uq': nrm(ks[14], (DEPTH, Q_LORA, N_HEADS * QK_DIM), Q_LORA ** -0.5),
        'w_ukv': nrm(ks[15], (DEPTH, KV_LORA, N_HEADS * (NOPE_DIM + V_DIM)), KV_LORA ** -0.5),
        'g_qn_nope': gain(ks[16], (DEPTH, NOPE_DIM)),
        'g_qn_rope': gain(ks[17], (DEPTH, ROPE_DIM)),
        'g_kn_nope': gain(ks[18], (DEPTH, NOPE_DIM)),
        'g_kn_rope': gain(ks[19], (DEPTH, ROPE_DIM)),
        'w_pool': nrm(ks[20], (DEPTH, POOL_GROUPS, POOL_GC, POOL_GC), POOL_GC ** -0.5),
        'pool_scale': gain(ks[21], (DEPTH, POOL_W)),
        'w_out': nrm(ks[22], (DEPTH, MIX_W, D), MIX_W ** -0.5),
        'w_ffn_gate': nrm(ks[23], (N_DENSE, D, D_FF), D ** -0.5),
        'w_ffn_up': nrm(ks[24], (N_DENSE, D, D_FF), D ** -0.5),
        'w_ffn_down': nrm(ks[25], (N_DENSE, D_FF, D), D_FF ** -0.5),
        'w_router': nrm(ks[26], (N_MOE, D, N_EXPERTS), D ** -0.5),
        'b_router': nrm(ks[27], (N_MOE, N_EXPERTS), 0.01),
        'w_exp_gate': nrm(ks[28], (N_MOE, N_EXPERTS, D, D_EXPERT), D ** -0.5),
        'w_exp_up': nrm(ks[29], (N_MOE, N_EXPERTS, D, D_EXPERT), D ** -0.5),
        'w_exp_down': nrm(ks[30], (N_MOE, N_EXPERTS, D_EXPERT, D), D_EXPERT ** -0.5),
    }

def reference(x_prompt, x_sample, c_prompt, c_sample, cache_ckv, cache_krope, state_pool,
              g_mix, g_ffn, w_ada, b_ada, w_in, g_q_lat, g_kv_lat, w_uq, w_ukv,
              g_qn_nope, g_qn_rope, g_kn_nope, g_kn_rope, w_pool, pool_scale, w_out,
              w_ffn_gate, w_ffn_up, w_ffn_down, w_router, b_router,
              w_exp_gate, w_exp_up, w_exp_down):
    xp, xs = x_prompt, x_sample
    ckv_p, kr_p, pool_p = [], [], []
    ckv_s, kr_s, pool_s = [], [], []
    for l in range(DEPTH):
        p = {
            'g_mix': g_mix[l], 'g_ffn': g_ffn[l], 'w_ada': w_ada[l], 'b_ada': b_ada[l],
            'w_in': w_in[l], 'g_q_lat': g_q_lat[l], 'g_kv_lat': g_kv_lat[l],
            'w_uq': w_uq[l], 'w_ukv': w_ukv[l],
            'g_qn_nope': g_qn_nope[l], 'g_qn_rope': g_qn_rope[l],
            'g_kn_nope': g_kn_nope[l], 'g_kn_rope': g_kn_rope[l],
            'w_pool': w_pool[l], 'pool_scale': pool_scale[l], 'w_out': w_out[l],
        }
        j = l // 2
        if l % 2 == 0:
            ffn = functools.partial(swiglu, wg=w_ffn_gate[j], wu=w_ffn_up[j], wd=w_ffn_down[j])
        else:
            ffn = functools.partial(moe_swiglu, w_router=w_router[j], b_router=b_router[j],
                                    wg=w_exp_gate[j], wu=w_exp_up[j], wd=w_exp_down[j])
        xp, a, b, cc = trunk_layer(xp, c_prompt, 0, None, None, None, p, ffn)
        xs, d, e, f = trunk_layer(xs, c_sample, PAST_LEN, cache_ckv[l], cache_krope[l],
                                  state_pool[l], p, ffn)
        ckv_p.append(a)
        kr_p.append(b)
        pool_p.append(cc)
        ckv_s.append(d)
        kr_s.append(e)
        pool_s.append(f)
    return (xp, xs,
            jnp.stack(ckv_p), jnp.stack(kr_p), jnp.stack(pool_p),
            jnp.stack(ckv_s), jnp.stack(kr_s), jnp.stack(pool_s))


_drawn_inputs = setup_inputs


def setup_inputs(seed=0):
    import zlib

    import numpy as np

    out = dict(_drawn_inputs(seed))
    spreads = {}
    factors = {'g_qn_rope': 8.0, 'b_router': 6.15, 'g_qn_nope': 2.926, 'g_kn_nope': 5.362}
    for name, (base, spread) in spreads.items():
        noise = np.random.default_rng([zlib.crc32(name.encode()), seed]).standard_normal(out[name].shape)
        drawn = base * np.exp(spread * noise) if base else spread * noise
        out[name] = __import__('jax').numpy.asarray(drawn.astype(out[name].dtype))
    for name, factor in factors.items():
        out[name] = (out[name] * factor).astype(out[name].dtype)
    return out
```

```python
from contextlib import ExitStack

import concourse.bass as bass
from concourse import mybir

ALU = mybir.AluOpType
ACT = mybir.ActivationFunctionType
F32 = mybir.dt.float32
U32 = mybir.dt.uint32
AX = mybir.AxisListType

P = 128
D = 1024
KD = D // P
T_P, T_S = 512, 64
T = T_P + T_S
HALF = T // 2
DEPTH = 2
PAST = 256
CHUNK = 64
NH = 8
Q_LORA, KV_LORA = 256, 128
NOPE, ROPE, VD = 64, 32, 64
QK = NOPE + ROPE
LAT = Q_LORA + KV_LORA + ROPE
POOL_G = 4
HIST = 15
N_EXP = 8
F_EXP = 1408
KF = F_EXP // P
N_DENSE_PARTS = 2
EPS = 1e-6
SCALE = QK ** -0.5
NEG = -1e30

TILES = [(t * P, min(P, T - t * P)) for t in range((T + P - 1) // P)]
KEYS = T_P + PAST + T_S
KTILES = [(t * P, min(P, KEYS - t * P)) for t in range((KEYS + P - 1) // P)]
NT, NKT = len(TILES), len(KTILES)
EXT = HIST + T_P + HIST + T_S
S_AT = HIST + T_P

SLOTS = 5
SLOT = 2 * KF * P
ADA_W = 256
ADA_N = 6 * D // ADA_W
MIX_N = 9
EXP_N = KF + KD // 2

UNITS = [(i, h) for i in range(NT) for h in range(NH)]


def layer_chunks(l):
    base = l * (ADA_N + MIX_N + N_DENSE_PARTS * EXP_N)
    return base, base + ADA_N, base + ADA_N + MIX_N


def build(nc, d, o):
    with ExitStack() as ctx:
        def sb(name, shape, dt=F32):
            return ctx.enter_context(nc.sbuf_tensor(name, shape, dt))

        def sem(name):
            return ctx.enter_context(nc.semaphore(name))

        PS = ctx.enter_context(nc.psum_tensor("PS", [P, 8, 512], F32))

        ring = sb("ring", [P, SLOTS, SLOT])
        x = sb("x", [P, KD, T])
        hT = sb("hT", [P, KD, T])
        work = sb("work", [P, NH * (T + KEYS) + NKT * 512])
        qT = work[0:QK, 0:NH * T].rearrange("p (h t) -> p h t", h=NH)
        kT = work[0:QK, NH * T:NH * (T + KEYS)].rearrange("p (h t) -> p h t", h=NH)
        V = work[:, NH * (T + KEYS):].rearrange("p (t n) -> p t n", t=NKT)
        mid = work[:, 0:KF * T].rearrange("p (f t) -> p f t", f=KF)
        combR = work[:, KF * T:(KF + N_EXP) * T].rearrange("p (e t) -> p e t", e=N_EXP)
        qlT = sb("qlT", [P, 2, T])
        ckvT = sb("ckvT", [P, KEYS])
        uE = sb("uE", [P, POOL_G, EXT])
        win = sb("win", [P, 2, EXT])
        dT = hT[:, 4:8, :]
        sg = win[:, :, 0:T]
        rstd = sb("rstd", [P, T])
        tok = sb("tok", [P, 2, NH * QK])
        sq = sb("sq", [P, 2, NH * QK])
        ropeA = sb("ropeA", [P, NH, ROPE])
        ropeB = sb("ropeB", [P, NH, ROPE])
        ropeX = sb("ropeX", [P, NH, ROPE])
        kr = sb("kr", [P, NKT, ROPE])
        prob, probT = sq[:, :, 0:512], tok[:, :, 0:512]
        stat = sb("stat", [P, 2, 16])
        rst = sb("rst", [P, 2, 16])
        nmax = sb("nmax", [P, 2])
        psumr = sb("psumr", [P, 2])
        rinv = sb("rinv", [P, 2])
        modrow = sb("modrow", [2, 5, ADA_W])
        mod = sb("mod", [P, 48, 2])
        amod = sb("amod", [P, 2, KD, 2])
        cT = sb("cT", [P, KD, 2])
        scT = sb("scT", [P, KD, 2])
        ident = sb("ident", [P, P])
        ones = sb("ones", [P, P])
        eps = sb("eps", [P, 1])
        cs = sb("cs", [P, 2, NT, ROPE])
        qtab = sb("qtab", [P, 2, NT, ROPE])
        ktab = sb("ktab", [P, 2, NT, ROPE])
        ptab = sb("ptab", [P, POOL_G, 16])
        bada = sb("bada", [P, DEPTH, 48])
        gmix = sb("gmix", [P, DEPTH, 2, KD])
        glat = sb("glat", [P, DEPTH, 3])
        g96 = sb("g96", [QK, DEPTH, 2])
        grow = sb("grow", [P, DEPTH, 2, ROPE])
        pscale = sb("pscale", [P, DEPTH, POOL_G])
        wr = sb("wr", [P, KD, N_EXP])
        br = sb("br", [P, N_EXP])
        logit = sb("logit", [P, NT, N_EXP])
        top = sb("top", [P, NT, 8])
        topi = sb("topi", [P, NT, 8], U32)
        topf = sb("topf", [P, NT, 8])
        iota8 = sb("iota8", [P, N_EXP])
        tw = sb("tw", [P, NT, 4])
        comb = sb("comb", [P, NT, N_EXP])
        comb2 = sb("comb2", [P, NT, N_EXP])

        const_in, x_in = sem("const_in"), sem("x_in")
        past_in = sem("past_in")
        out_sem = sem("stored")
        slot_full = [sem(f"slot_full{i}") for i in range(SLOTS)]
        setup = sem("setup")
        gains_set = sem("gains_set")
        silu_c = sem("silu_c")
        ada_done, row_done, modT_done, mod_done = sem("ada_done"), sem("row_done"), sem("modT_done"), sem("mod_done")
        tab_done = sem("tab_done")
        squared, ssum_done, ms_done, rms_done, hn_done = sem("squared"), sem("ssum_done"), sem("ms_done"), sem("rms_done"), sem("hn_done")
        h_prompt, h_sample = sem("h_prompt"), sem("h_sample")
        z_done, z_stat, zn_done, lat_T, lat_done = sem("z_done"), sem("z_stat"), sem("zn_done"), sem("lat_T"), sem("lat_done")
        kr_done = sem("kr_done")
        u_done, u_copied, win_done, d_done, pool_done, pool_copied = (
            sem("u_done"), sem("u_copied"), sem("win_done"), sem("d_done"), sem("pool_done"), sem("pool_copied"))
        qk_done, qk_sq, qk_sum, qk_rms, qk_norm, krc_done, qk_T, qk_copied = (
            sem("qk_done"), sem("qk_sq"), sem("qk_sum"), sem("qk_rms"), sem("qk_norm"), sem("krc_done"), sem("qk_T"), sem("qk_copied"))
        v_copied = sem("v_copied")
        s_done, max_done, exp_done, p_done, pT_done, pT_copied, pv_done, o_copied = (
            sem("s_done"), sem("max_done"), sem("exp_done"), sem("p_done"), sem("pT_done"), sem("pT_copied"), sem("pv_done"), sem("o_copied"))
        y_done, x_done = sem("y_done"), sem("x_done")
        gate_done, up_done, silu_done, sgc_done, mid_done, down_done, acc_done = (
            sem("gate_done"), sem("up_done"), sem("silu_done"), sem("sgc_done"), sem("mid_done"), sem("down_done"), sem("acc_done"))
        lg_done, top_done, tw_done, comb_done, cr_done, cr_copied = (
            sem("lg_done"), sem("top_done"), sem("tw_done"), sem("comb_done"), sem("cr_done"), sem("cr_copied"))
        act_chain, dve_chain, pool_chain = sem("act_chain"), sem("dve_chain"), sem("pool_chain")

        PARTS = N_DENSE_PARTS + N_EXP

        def parts(l):
            return (0, N_DENSE_PARTS) if l % 2 == 0 else (N_DENSE_PARTS, N_EXP)

        QKT = NT + NKT
        CONSTS = 17
        block = ctx.enter_context(nc.Block())

        class Chain:
            def __init__(self, eng, s):
                self.eng, self.s, self.n = eng, s, 0

            def step(self, ins):
                ins.then_inc(self.s, 1)
                self.n += 1

            def sync(self):
                self.eng.wait_ge(self.s, self.n)

        @block.sync
        def _(sp):
            def ffn_release(e, c):
                return (up_done, e * KF + c + 1) if c < KF else (down_done, e * KD + 2 * (c - KF) + 2)

            release = []
            for l in range(DEPTH):
                release += [(ada_done, ADA_N * l + j + 1) for j in range(ADA_N)]
                release += [(z_done, NT * (l + 1)), (pool_done, POOL_G * (l + 1))]
                release += [(u_done, POOL_G * l + 2 * j + 2) for j in range(2)]
                release += [(qk_done, QKT * (l + 1))]
                release += [(y_done, KD * l + 2 * j + 2) for j in range(4)]
                release += [ffn_release(parts(l)[0] + i, c) for i in range(parts(l)[1]) for c in range(EXP_N)]

            def fill(g, src, n, after=None):
                if after is None and g >= SLOTS:
                    after = release[g - SLOTS]
                if after is not None:
                    sp.wait_ge(*after)
                sp.dma_start(ring[:, g % SLOTS, 0:n], src).then_inc(slot_full[g % SLOTS], 16)

            sp.dma_start(cT[:], d["c"]).then_inc(const_in, 16)
            fill(0, d["ada"][0, 0], KD * ADA_W)
            sp.dma_start(x[:], d["x"]).then_inc(x_in, 16)
            for dst, src in ((ident, "ident"), (cs, "cs"), (ptab, "ptab"), (bada, "b_ada"), (gmix, "g_norm"),
                             (glat, "g_lat"), (pscale, "pool_scale"), (wr, "w_router"), (iota8, "iota8")):
                sp.dma_start(dst[:], d[src]).then_inc(const_in, 16)
            for l in range(DEPTH):
                sp.dma_start(g96[0:NOPE, l, :], d["g_nope"][l]).then_inc(const_in, 16)
                for j in range(2):
                    sp.dma_start(grow[:, l, j, :], d["g_rope"][l, j].partition_broadcast(P)).then_inc(const_in, 16)
            sp.dma_start(br[:], d["b_router"].partition_broadcast(P)).then_inc(const_in, 16)
            for j in range(2):
                sp.dma_start(kr[:, 4 + j, :], d["krope"][0, j]).then_inc(past_in, 16)
            sp.dma_start(ckvT[:, T_P:T_P + PAST], d["ckv"][0]).then_inc(past_in, 16)
            sp.dma_start(uE[:, :, S_AT:S_AT + HIST], d["hist"][0]).then_inc(past_in, 16)
            for l in range(DEPTH):
                g_ada, g_mix, g_ffn = layer_chunks(l)
                for j in range(1 if l == 0 else 0, 5):
                    fill(g_ada + j, d["ada"][l, j], KD * ADA_W)
                with sp.Fori(1, ADA_N // 5) as i:
                    for j in range(5):
                        fill(g_ada + j, d["ada"][l, bass.ds(i * 5 + j, 1)].rearrange("a p n -> p (a n)"),
                             KD * ADA_W, after=(ada_done, ADA_N * l + (i - 1) * 5 + j + 1))
                for j in range(ADA_N - ADA_N % 5, ADA_N):
                    fill(g_ada + j, d["ada"][l, j], KD * ADA_W)
                mix = [(d["w_t0"][l], 4 * LAT), (d["w_t1"][l], 4 * LAT + POOL_G * P)]
                mix += [(d["w_u"][l, j], 2 * D) for j in range(2)]
                mix += [(d["w_q"][l], 2 * NH * QK + 2 * 512)]
                mix += [(d["w_o"][l, j], 2 * D) for j in range(4)]
                for j, (src, n) in enumerate(mix):
                    fill(g_mix + j, src, n)
                    if l == 1 and j == 0:
                        sp.wait_ge(qk_copied, 2 * QKT)
                        sp.wait_ge(out_sem, 16 * 6)
                        for b in range(2):
                            sp.dma_start(kr[:, 4 + b, :], d["krope"][1, b]).then_inc(past_in, 16)
                        sp.dma_start(ckvT[:, T_P:T_P + PAST], d["ckv"][1]).then_inc(past_in, 16)
                        sp.wait_ge(d_done, 4)
                        sp.dma_start(uE[:, :, S_AT:S_AT + HIST], d["hist"][1]).then_inc(past_in, 16)
                    if j == 4:
                        sp.wait_ge(lat_done, NT * (l + 1))
                        sp.dma_start(o["ckv"][l, :, 0:T_P], ckvT[:, 0:T_P]).then_inc(out_sem, 16)
                        sp.dma_start(o["ckv"][l, :, T_P:T], ckvT[:, T_P + PAST:KEYS]).then_inc(out_sem, 16)
                        sp.wait_ge(kr_done, NT * (l + 1))
                        sp.dma_start(o["krope"][l, :, 0:4, :], kr[:, 0:4, :]).then_inc(out_sem, 16)
                        sp.dma_start(o["krope"][l, 0:T_S, 4, :], kr[0:T_S, NKT - 1, :]).then_inc(out_sem, 16)
                        sp.wait_ge(u_copied, POOL_G * 3 * (l + 1))
                        sp.dma_start(o["pool"][l, :, :, 0, :], uE[:, :, S_AT - HIST:S_AT]).then_inc(out_sem, 16)
                        sp.dma_start(o["pool"][l, :, :, 1, :], uE[:, :, EXT - HIST:EXT]).then_inc(out_sem, 16)
                w_gu, w_dn = (d["w_gu"], d["w_dn"]) if l == 0 else (d["e_gu"], d["e_dn"])
                width = lambda c: 2 * D if c < KF else SLOT
                for c in range(EXP_N):
                    fill(g_ffn + c, w_gu[0, c] if c < KF else w_dn[0, c - KF], width(c))
                with sp.Fori(1, parts(l)[1]) as i:
                    e = i + parts(l)[0]
                    for c in range(EXP_N):
                        src = w_gu[bass.ds(i, 1), c] if c < KF else w_dn[bass.ds(i, 1), c - KF]
                        fill(g_ffn + c, src.rearrange("a p n -> p (a n)"), width(c),
                             after=ffn_release(e, c - SLOTS) if c >= SLOTS else ffn_release(e - 1, c - SLOTS + EXP_N))
            sp.wait_ge(acc_done, KD * PARTS + 1)
            sp.dma_start(o["y"], x[:]).then_inc(out_sem, 16)
            sp.wait_ge(out_sem, 16 * (6 * DEPTH + 1))

        @block.tensor
        def _(pe):
            def have(g, use=None):
                pe.wait_ge(slot_full[g % SLOTS], 16 * (g // SLOTS + 1) if use is None else (use + 1) * 16)

            def rms_sum(n):
                pe.wait_ge(ssum_done, n + 1)
                for h in range(2):
                    mm = pe.matmul(PS[:, 6 + h, 0:HALF], ones[:], rstd[:, h * HALF:(h + 1) * HALF], start=True, stop=True)
                mm.then_inc(ms_done, 1)

            def ada_chunk(l, j, jj, use, n, first):
                g = layer_chunks(l)[0] + jj
                have(g, use)
                if not first:
                    pe.wait_ge(row_done, n - 4)
                for k in range(KD):
                    mm = pe.matmul(PS[0:2, [0, 1, 3, 4, 5][jj % 5], 0:ADA_W], scT[:, k, :],
                                   ring[:, g % SLOTS, k * ADA_W:(k + 1) * ADA_W], start=(k == 0), stop=(k == KD - 1))
                mm.then_inc(ada_done, 1)

            def ada_turn(l, j, jj, n):
                pe.wait_ge(row_done, n + 1)
                for b in range(2):
                    at = j * 4 + b * 2
                    dst = PS[:, 2, at:at + 2] if isinstance(at, int) else PS[:, 2, bass.ds(at, 2)]
                    mm = pe.matmul(dst, modrow[:, jj % 5, b * P:(b + 1) * P], ident[0:2, 0:2],
                                   start=True, stop=True)
                mm.then_inc(modT_done, 1)

            def ada(l):
                n0 = l * ADA_N
                if l == 0:
                    pe.wait_ge(silu_c, 1)
                    pe.wait_ge(const_in, 16 * CONSTS)
                else:
                    pe.wait_ge(acc_done, KD * N_DENSE_PARTS + 1)
                base = layer_chunks(l)[0]

                def five(i, count, first):
                    for jj in range(count):
                        j = i * 5 + jj
                        ada_chunk(l, j, jj, None if isinstance(i, int) and False else i + (base + jj) // SLOTS, j + n0, first)
                    for jj in range(count):
                        ada_turn(l, i * 5 + jj, jj, i * 5 + jj + n0)
                five(0, 5, True)
                with pe.Fori(1, ADA_N // 5) as i:
                    five(i, 5, False)
                five(ADA_N // 5, ADA_N % 5, False)

            def mixer(l):
                g = layer_chunks(l)[1]
                pe.wait_ge(h_prompt, KD * (2 * l + 1))
                pe.wait_ge(h_sample, KD * (2 * l + 1))

                def latents(t):
                    at, n = TILES[t]
                    if t >= 2:
                        pe.wait_ge(kr_done, NT * l + t - 1)
                    for k in range(KD):
                        w = ring[:, (g + k // 4) % SLOTS, (k % 4) * LAT:(k % 4 + 1) * LAT]
                        if t == 0 and k % 4 == 0:
                            have(g + k // 4)
                        mm = pe.matmul(PS[0:n, t % 2, 0:LAT], hT[:, k, at:at + n], w, start=(k == 0), stop=(k == KD - 1))
                    mm.then_inc(z_done, 1)

                def latents_turn(t):
                    at, n = TILES[t]
                    pe.wait_ge(zn_done, NT * l + t + 1)
                    if t >= 2:
                        pe.wait_ge(lat_done, NT * l + t - 1)
                    for b in range(3):
                        mm = pe.transpose(PS[:, 2 + t % 2, b * P:b * P + n], tok[0:n, t % 2, b * P:(b + 1) * P], ident[0:n, 0:n])
                    mm.then_inc(lat_T, 1)

                for t in range(NT):
                    latents(t)
                    if t >= 1:
                        latents_turn(t - 1)
                latents_turn(NT - 1)
                for b in range(POOL_G):
                    s = (g + 2 + b // 2) % SLOTS
                    if b % 2 == 0:
                        have(g + 2 + b // 2)
                    if b >= 2:
                        pe.wait_ge(u_copied, 3 * (POOL_G * l + b - 1))
                    for h in range(2):
                        for k in range(KD):
                            mm = pe.matmul(PS[:, 4 + 2 * (b % 2) + h, 0:HALF], ring[:, s, (b % 2) * D + k * P:(b % 2) * D + (k + 1) * P],
                                           hT[:, k, h * HALF:(h + 1) * HALF], start=(k == 0), stop=(k == KD - 1))
                    mm.then_inc(u_done, 1)
                have(g + 4)
                wq = ring[:, (g + 4) % SLOTS, 0:2 * NH * QK].rearrange("p (k n) -> p k n", k=2)
                wk = ring[:, (g + 4) % SLOTS, 2 * NH * QK:2 * NH * QK + 1024]
                pe.wait_ge(lat_done, NT * (l + 1))
                pe.wait_ge(kr_done, NT * (l + 1))
                pe.wait_ge(past_in, 64 * (l + 1))

                def project(j):
                    b0 = 2 * (j % 2)
                    if j >= 2:
                        pe.wait_ge(qk_norm, QKT * l + j - 1)
                        if j >= NT + 2:
                            pe.wait_ge(v_copied, NKT * l + j - NT - 1)
                    if j < NT:
                        at, n = TILES[j]
                        for h in range(2):
                            for k in range(2):
                                mm = pe.matmul(PS[0:n, b0 + h, 0:384], qlT[:, k, at:at + n], wq[:, k, h * 384:(h + 1) * 384],
                                               start=(k == 0), stop=(k == 1))
                    else:
                        at, n = KTILES[j - NT]
                        for h in range(2):
                            mm = pe.matmul(PS[0:n, b0 + h, :], ckvT[:, at:at + n], wk[:, h * 512:(h + 1) * 512], start=True, stop=True)
                    mm.then_inc(qk_done, 1)

                def heads_turn(j):
                    at, n = TILES[j] if j < NT else KTILES[j - NT]
                    pe.wait_ge(qk_norm, QKT * l + j + 1)
                    if j >= NT:
                        pe.wait_ge(krc_done, NKT * l + j - NT + 1)
                    if j >= 2:
                        pe.wait_ge(qk_copied, 2 * (QKT * l + j - 1))
                    else:
                        pe.wait_ge(u_copied, 3 * POOL_G * (l + 1))
                    for h in range(NH):
                        mm = pe.transpose(PS[0:QK, 4 + 2 * (j % 2) + h // 4, (h % 4) * P:(h % 4) * P + n],
                                          tok[0:n, j % 2, h * QK:(h + 1) * QK], ident[0:n, 0:n])
                    mm.then_inc(qk_T, 1)

                for j in range(QKT):
                    project(j)
                    if j >= 1:
                        heads_turn(j - 1)
                heads_turn(QKT - 1)
                pe.wait_ge(qk_copied, 2 * QKT * (l + 1))
                for b in range(POOL_G):
                    pe.wait_ge(d_done, POOL_G * l + b + 1)
                    if b >= 2:
                        pe.wait_ge(pool_copied, POOL_G * l + b - 1)
                    for h in range(2):
                        mm = pe.matmul(PS[:, 4 + 2 * (b % 2) + h, 0:HALF], ring[:, (g + 1) % SLOTS, 4 * LAT + b * P:4 * LAT + (b + 1) * P],
                                       dT[:, b, h * HALF:(h + 1) * HALF], start=True, stop=True)
                    mm.then_inc(pool_done, 1)
                pe.wait_ge(pool_copied, POOL_G * (l + 1))
                U = len(UNITS)

                def scores(u):
                    i, h = UNITS[u]
                    at, n = TILES[i]
                    k0, nk = (0, at + P) if i < 4 else (T_P, PAST + T_S)
                    if u >= 2:
                        pe.wait_ge(exp_done, U * l + u - 1)
                    else:
                        pe.wait_ge(v_copied, NKT * (l + 1))
                    pe.matmul(PS[0:n, u % 2, 0:nk], qT[:, h, at:at + n], kT[:, h, k0:k0 + nk], start=True, stop=True).then_inc(s_done, 1)

                def key_blocks(i):
                    return [(b, b, P) for b in range(i + 1)] if i < 4 else [(b, 4 + b, KTILES[4 + b][1]) for b in range(3)]

                def probs_turn(u):
                    i, h = UNITS[u]
                    n = TILES[i][1]
                    pe.wait_ge(p_done, U * l + u + 1)
                    if u >= 2:
                        pe.wait_ge(pT_copied, U * l + u - 1)
                    for b, kb, nk in key_blocks(i):
                        mm = pe.transpose(PS[0:nk, 2 + u % 2, b * P:b * P + n], prob[0:n, u % 2, b * P:b * P + nk], ident[0:n, 0:n])
                    mm.then_inc(pT_done, 1)

                def values(u):
                    i, h = UNITS[u]
                    n = TILES[i][1]
                    pe.wait_ge(pT_copied, U * l + u + 1)
                    if h == 0 and i >= 2:
                        pe.wait_ge(o_copied, NT * l + i - 1)
                    r = (h % 2) * VD
                    kb_ = key_blocks(i)
                    for m, (b, kb, nk) in enumerate(kb_):
                        mm = pe.matmul(PS[r:r + VD, 4 + i % 2, (h // 2) * P:(h // 2) * P + n], V[0:nk, kb, h * VD:(h + 1) * VD],
                                       probT[0:nk, u % 2, b * P:b * P + n], start=(m == 0), stop=(m == len(kb_) - 1))
                    mm.then_inc(pv_done, 1)

                for u in range(U + 2):
                    if u < U:
                        scores(u)
                    if 1 <= u <= U:
                        probs_turn(u - 1)
                    if u >= 2:
                        values(u - 2)
                pe.wait_ge(o_copied, NT * (l + 1))
                for m in range(KD):
                    s = (g + 5 + m // 2) % SLOTS
                    if m % 2 == 0:
                        have(g + 5 + m // 2)
                    if m >= 4:
                        pe.wait_ge(x_done, KD * l + m - 3)
                    for h in range(2):
                        for k in range(KD):
                            mm = pe.matmul(PS[:, 2 * (m % 4) + h, 0:HALF], ring[:, s, (m % 2) * D + k * P:(m % 2) * D + (k + 1) * P],
                                           hT[:, k, h * HALF:(h + 1) * HALF], start=(k == 0), stop=(k == KD - 1))
                    mm.then_inc(y_done, 1)

            def ffn(l):
                g = layer_chunks(l)[2]
                e0, ne = parts(l)
                pe.wait_ge(h_prompt, KD * (2 * l + 2))
                pe.wait_ge(h_sample, KD * (2 * l + 2))
                if l == 1:
                    for t, (at, n) in enumerate(TILES):
                        for k in range(KD):
                            mm = pe.matmul(PS[0:n, 0, t * N_EXP:(t + 1) * N_EXP], hT[:, k, at:at + n], wr[:, k, :],
                                           start=(k == 0), stop=(k == KD - 1))
                    mm.then_inc(lg_done, 1)
                    pe.wait_ge(comb_done, 1)
                    for e in range(N_EXP):
                        if e >= 3:
                            pe.wait_ge(cr_copied, e - 2)
                        for t, (at, n) in enumerate(TILES):
                            h, c = (0, at) if at < T_P else (1, 0)
                            mm = pe.matmul(PS[:, 2 * (e % 3) + 2 + h, c:c + n], comb[0:n, t, e:e + 1].to_broadcast([n, P]), ident[0:n, 0:n],
                                           start=True, stop=True)
                        mm.then_inc(cr_done, 1)
                    pe.wait_ge(cr_copied, N_EXP)
                with pe.Fori(0, ne) as i:
                    e = i + e0
                    use = i * (EXP_N // SLOTS)
                    for c in range(KF):
                        have(g + c, use + (g + c) // SLOTS)
                        b0 = 4 * (c % 2)
                        if c >= 2:
                            pe.wait_ge(mid_done, e * KF + c - 1)
                        else:
                            pe.wait_ge(acc_done, e * KD + 1)
                        s = (g + c) % SLOTS
                        for w, done in ((0, gate_done), (1, up_done)):
                            for h in range(2):
                                for k in range(KD):
                                    mm = pe.matmul(PS[:, b0 + 2 * w + h, 0:HALF], ring[:, s, w * D + k * P:w * D + (k + 1) * P],
                                                   hT[:, k, h * HALF:(h + 1) * HALF], start=(k == 0), stop=(k == KD - 1))
                            mm.then_inc(done, 1)
                    pe.wait_ge(mid_done, e * KF + KF)
                    for m in range(KD):
                        s = (g + KF + m // 2) % SLOTS
                        if m % 2 == 0:
                            have(g + KF + m // 2, use + (g + KF + m // 2) // SLOTS)
                        if m >= 4:
                            pe.wait_ge(acc_done, e * KD + m - 3 + 1)
                        for h in range(2):
                            for f in range(KF):
                                at = (m % 2) * KF * P + f * P
                                mm = pe.matmul(PS[:, 2 * (m % 4) + h, 0:HALF], ring[:, s, at:at + P],
                                               mid[:, f, h * HALF:(h + 1) * HALF], start=(f == 0), stop=(f == KF - 1))
                        mm.then_inc(down_done, 1)

            for l in range(DEPTH):
                ada(l)
                rms_sum(2 * l)
                mixer(l)
                rms_sum(2 * l + 1)
                ffn(l)

        @block.scalar
        def _(act):
            chain = Chain(act, act_chain)

            def norm(n):
                l, which = n // 2, n % 2
                if n == 0:
                    act.wait_ge(x_in, 16)
                    act.wait_ge(setup, 1)
                elif which == 1:
                    act.wait_ge(x_done, KD * (l + 1))
                else:
                    act.wait_ge(acc_done, KD * N_DENSE_PARTS + 1)
                act.activation(hT[:], x[:], ACT.Square).then_inc(squared, 1)
                act.wait_ge(ms_done, n + 1)
                act.activation(rstd[:].rearrange("p (h t) -> p h t", h=2), PS[:, 6:8, 0:HALF], ACT.Sqrt,
                               bias=eps[:], scale=1.0 / D).then_inc(rms_done, 1)
                act.wait_ge(mod_done, 3 * (l + 1))
                for k in range(KD):
                    act.wait_ge(hn_done, KD * n + k + 1)
                    act.activation(hT[:, k, 0:T_P], hT[:, k, 0:T_P], ACT.Identity, bias=mod[:, 24 * which + k, 0:1],
                                   scale=amod[:, which, k, 0:1]).then_inc(h_prompt, 1)

            def ada(l):
                def copy(j, jj, n, first):
                    act.wait_ge(ada_done, n + 1)
                    if not first:
                        act.wait_ge(modT_done, n - 4)
                    act.copy(modrow[:, jj % 5, :], PS[0:2, [0, 1, 3, 4, 5][jj % 5], 0:ADA_W]).then_inc(row_done, 1)
                n0 = l * ADA_N
                for jj in range(5):
                    copy(jj, jj, n0 + jj, l == 0)
                with act.Fori(1, ADA_N // 5) as i:
                    for jj in range(5):
                        copy(i * 5 + jj, jj, i * 5 + jj + n0, False)
                for j in range(ADA_N - ADA_N % 5, ADA_N):
                    copy(j, j, n0 + j, False)

            def mixer(l):
                for t, (at, n) in enumerate(TILES):
                    act.wait_ge(z_done, NT * l + t + 1)
                    if t >= 2 or l > 0:
                        act.wait_ge(kr_done, NT * l + t - 1)
                    b = t % 2
                    for j, (c0, w) in enumerate(((0, Q_LORA), (Q_LORA, KV_LORA), (Q_LORA + KV_LORA, ROPE))):
                        chain.step(act.activation(sq[0:n, b, c0:c0 + w], PS[0:n, b, c0:c0 + w], ACT.Square,
                                                  scale=float(w) ** -0.5, accum_out=stat[0:n, b, j:j + 1]))
                    chain.sync()
                    act.activation(rst[0:n, b, 0:3], stat[0:n, b, 0:3], ACT.Sqrt, bias=eps[0:n, :]).then_inc(z_stat, 1)
                    if t >= 1:
                        latents_out(l, t - 1)
                latents_out(l, NT - 1)
                for b in range(POOL_G):
                    act.wait_ge(u_done, POOL_G * l + b + 1)
                    if b == 0:
                        act.wait_ge(win_done, POOL_G * l) if l else None
                        act.wait_ge(d_done, POOL_G * l) if l else None
                        act.wait_ge(out_sem, 16 * 6 * l) if l else None
                    b0 = 4 + 2 * (b % 2)
                    act.copy(uE[:, b, HIST:HIST + HALF], PS[:, b0, 0:HALF]).then_inc(u_copied, 1)
                    act.copy(uE[:, b, HIST + HALF:HIST + T_P], PS[:, b0 + 1, 0:T_P - HALF]).then_inc(u_copied, 1)
                    act.copy(uE[:, b, S_AT + HIST:EXT], PS[:, b0 + 1, T_P - HALF:HALF]).then_inc(u_copied, 1)
                for j in range(QKT):
                    n = TILES[j][1] if j < NT else KTILES[j - NT][1]
                    b0 = 2 * (j % 2)
                    act.wait_ge(qk_done, QKT * l + j + 1)
                    if j >= 2:
                        act.wait_ge(qk_sum, QKT * l + j - 1)
                    if j < NT:
                        act.activation(sq[0:n, j % 2, :].rearrange("p (h n) -> p h n", h=2), PS[0:n, b0:b0 + 2, 0:384],
                                       ACT.Square).then_inc(qk_sq, 1)
                    else:
                        act.activation(sq[0:n, j % 2, 0:512], PS[0:n, b0, :], ACT.Square).then_inc(qk_sq, 1)
                        act.copy(V[0:n, j - NT, :], PS[0:n, b0 + 1, :]).then_inc(v_copied, 1)
                    act.wait_ge(qk_sum, QKT * l + j + 1)
                    chain.step(act.activation(rst[0:n, j % 2, 0:8], stat[0:n, j % 2, 0:8], ACT.Sqrt, bias=eps[0:n, :], scale=1.0 / NOPE))
                    act.activation(rst[0:n, j % 2, 8:16], stat[0:n, j % 2, 8:16], ACT.Sqrt, bias=eps[0:n, :],
                                   scale=1.0 / ROPE).then_inc(qk_rms, 1)
                    if j >= 1:
                        heads_out(l, j - 1)
                heads_out(l, QKT - 1)
                for b in range(POOL_G):
                    act.wait_ge(pool_done, POOL_G * l + b + 1)
                    b0 = 4 + 2 * (b % 2)
                    act.activation(hT[:, 4 + b, :].rearrange("p (h t) -> p h t", h=2), PS[:, b0:b0 + 2, 0:HALF], ACT.Copy,
                                   scale=pscale[:, l, b:b + 1]).then_inc(pool_copied, 1)
                U = len(UNITS)

                def copy_probs(u):
                    i, h = UNITS[u]
                    n = TILES[i][1]
                    act.wait_ge(pT_done, U * l + u + 1)
                    if u >= 2:
                        act.wait_ge(pv_done, U * l + u - 1)
                    if i < 4:
                        w = (i + 1) * P
                        act.copy(probT[:, u % 2, 0:w], PS[:, 2 + u % 2, 0:w]).then_inc(pT_copied, 1)
                    else:
                        v = lambda b, n_, lo, hi: b[0:n_, lo * P:hi * P].rearrange("p (b t) -> p b t", t=P)[:, :, 0:n]
                        chain.step(act.copy(v(probT[:, u % 2, :], P, 0, 2), v(PS[:, 2 + u % 2, :], P, 0, 2)))
                        act.copy(v(probT[:, u % 2, :], T_S, 2, 3), v(PS[:, 2 + u % 2, :], T_S, 2, 3)).then_inc(pT_copied, 1)

                for u in range(U + 1):
                    if u < U:
                        i, h = UNITS[u]
                        at, n = TILES[i]
                        nk = at + P if i < 4 else PAST + T_S
                        act.wait_ge(max_done, U * l + u + 1)
                        if u >= 2:
                            act.wait_ge(pT_done, U * l + u - 1)
                        act.activation(prob[0:n, u % 2, 0:nk], PS[0:n, u % 2, 0:nk], ACT.Exp, bias=nmax[0:n, u % 2:u % 2 + 1],
                                       accum_out=psumr[0:n, u % 2:u % 2 + 1]).then_inc(exp_done, 1)
                    if u >= 1:
                        copy_probs(u - 1)

            def latents_out(l, t):
                at, n = TILES[t]
                kat = at if t < 4 else T_P + PAST
                act.wait_ge(lat_T, NT * l + t + 1)
                for b in range(2):
                    chain.step(act.activation(qlT[:, b, at:at + n], PS[:, 2 + t % 2, b * P:b * P + n], ACT.Copy, scale=glat[:, l, b:b + 1]))
                if l == 1 and t == 0:
                    act.wait_ge(out_sem, 16 * 6)
                act.activation(ckvT[:, kat:kat + n], PS[:, 2 + t % 2, 2 * P:2 * P + n], ACT.Copy, scale=glat[:, l, 2:3]).then_inc(lat_done, 1)

            def heads_out(l, j):
                at, n = TILES[j] if j < NT else KTILES[j - NT]
                act.wait_ge(qk_T, QKT * l + j + 1)
                dst = (qT if j < NT else kT)[:, :, at:at + n]
                for h in range(2):
                    src = PS[0:QK, 4 + 2 * (j % 2) + h, :].rearrange("p (b t) -> p b t", b=4)[:, :, 0:n]
                    act.activation(dst[:, 4 * h:4 * h + 4, :], src, ACT.Copy,
                                   scale=g96[:, l, (0 if j < NT else 1):(1 if j < NT else 2)]).then_inc(qk_copied, 1)

            def ffn(l):
                e0, ne = parts(l)
                if l == 1:
                    act.wait_ge(tw_done, 1)
                    act.activation(tw[:, :, 1:2], tw[:, :, 0:1], ACT.Exp).then_inc(top_done, 1)
                    for e in range(N_EXP):
                        act.wait_ge(cr_done, e + 1)
                        b0 = 2 * (e % 3) + 2
                        chain.step(act.copy(combR[:, e, 0:T_P], PS[:, b0, 0:T_P]))
                        act.copy(combR[:, e, T_P:T], PS[:, b0 + 1, 0:T_S]).then_inc(cr_copied, 1)
                with act.Fori(0, ne) as i:
                    e = i + e0
                    for c in range(KF):
                        act.wait_ge(gate_done, e * KF + c + 1)
                        if c >= 2:
                            act.wait_ge(mid_done, e * KF + c - 1)
                        b0 = 4 * (c % 2)
                        act.activation(sg[:, c % 2, :].rearrange("p (h t) -> p h t", h=2), PS[:, b0:b0 + 2, 0:HALF],
                                       ACT.Silu).then_inc(silu_done, 1)

            act.wait_ge(const_in, 16 * CONSTS)
            act.activation(scT[:], cT[:], ACT.Silu).then_inc(silu_c, 1)
            act.wait_ge(gains_set, 2)
            for l in range(DEPTH):
                ada(l)
                norm(2 * l)
                mixer(l)
                norm(2 * l + 1)
                ffn(l)

        @block.vector
        def _(dve):
            chain = Chain(dve, dve_chain)

            def norm(n):
                dve.wait_ge(squared, n + 1)
                dve.tensor_reduce(rstd[:], hT[:].rearrange("p k t -> p t k"), AX.X, ALU.add).then_inc(ssum_done, 1)
                dve.wait_ge(rms_done, n + 1)
                chain.step(dve.reciprocal(rstd[:], rstd[:]))
                chain.sync()
                for k in range(KD):
                    dve.tensor_tensor(hT[:, k, :], x[:, k, :], rstd[:], ALU.mult).then_inc(hn_done, 1)

            def modulation(l):
                dve.wait_ge(modT_done, ADA_N * (l + 1))
                if l:
                    dve.wait_ge(h_sample, KD * 2 * l)
                dve.tensor_tensor(mod[:], PS[:, 2, 0:96].rearrange("p (m c) -> p m c", c=2),
                                  bada[:, l, :].unsqueeze(2).to_broadcast([P, 48, 2]), ALU.add).then_inc(mod_done, 1)
                dve.wait_ge(mod_done, 3 * l + 1)
                for j in range(2):
                    dve.scalar_tensor_tensor(out=amod[:, j], in0=mod[:, 24 * j + 8:24 * j + 16, :], scalar=1.0,
                                             in1=gmix[:, l, j, :].unsqueeze(2).to_broadcast([P, KD, 2]),
                                             op0=ALU.add, op1=ALU.mult).then_inc(mod_done, 1)

            def add_gated(bank, m, gate, last_sem):
                for h, c0, c1, a, cond in ((0, 0, HALF, 0, 0), (1, 0, T_P - HALF, HALF, 0), (1, T_P - HALF, HALF, T_P, 1)):
                    w = x[:, m, a:a + c1 - c0]
                    ins = dve.scalar_tensor_tensor(out=w, in0=PS[:, bank + h, c0:c1], scalar=mod[:, gate + m, cond:cond + 1],
                                                   in1=w, op0=ALU.mult, op1=ALU.add)
                ins.then_inc(last_sem, 1)

            def rotate(dst, src, tab, t, n, heads):
                cos = tab[0:n, 0, t, :].unsqueeze(1).to_broadcast([n, heads, ROPE])
                sin = tab[0:n, 1, t, :].unsqueeze(1).to_broadcast([n, heads, ROPE])
                hr = ROPE // 2
                A, B = ropeA[0:n, 0:heads, :], ropeB[0:n, 0:heads, :]
                chain.step(dve.tensor_tensor(A, src, cos, ALU.mult))
                chain.step(dve.tensor_tensor(B[:, :, 0:hr], src[:, :, hr:ROPE], sin[:, :, 0:hr], ALU.mult))
                chain.step(dve.tensor_tensor(B[:, :, hr:ROPE], src[:, :, 0:hr], sin[:, :, hr:ROPE], ALU.mult))
                chain.sync()
                return dve.tensor_tensor(dst, A, B, ALU.add)

            def mixer(l):
                dve.wait_ge(tab_done, 6 * (l + 1))
                for t, (at, n) in enumerate(TILES):
                    b = t % 2
                    dve.wait_ge(z_stat, NT * l + t + 1)
                    chain.step(dve.reciprocal(rst[0:n, b, 0:3], rst[0:n, b, 0:3]))
                    chain.sync()
                    if t >= 2:
                        dve.wait_ge(lat_T, NT * l + t - 1)
                    chain.step(dve.tensor_scalar(tok[0:n, b, 0:Q_LORA], PS[0:n, b, 0:Q_LORA], rst[0:n, b, 0:1], None, ALU.mult))
                    dve.tensor_scalar(tok[0:n, b, Q_LORA:Q_LORA + KV_LORA], PS[0:n, b, Q_LORA:Q_LORA + KV_LORA], rst[0:n, b, 1:2],
                                      None, ALU.mult).then_inc(zn_done, 1)
                    chain.step(dve.tensor_scalar(ropeX[0:n, 0, :], PS[0:n, b, Q_LORA + KV_LORA:LAT], rst[0:n, b, 2:3], None, ALU.mult))
                    chain.sync()
                    kt = t if t < 4 else NKT - 1
                    if l == 1 and t == 0:
                        dve.wait_ge(out_sem, 16 * 6)
                        dve.wait_ge(krc_done, NKT)
                    rotate(kr[0:n, kt:kt + 1, :], ropeX[0:n, 0:1, :], ktab, t, n, 1).then_inc(kr_done, 1)
                for b in range(POOL_G):
                    if b == 0:
                        dve.wait_ge(u_copied, 3 * POOL_G * (l + 1))
                    w = 2 << b
                    dve.wait_ge(win_done, POOL_G * l + b + 1)
                    s = win[:, b % 2, :]
                    chain.step(dve.scalar_tensor_tensor(out=dT[:, b, 0:T_P], in0=s[:, HIST:S_AT], scalar=1.0 / w, in1=uE[:, b, HIST:S_AT],
                                                        op0=ALU.mult, op1=ALU.subtract))
                    dve.scalar_tensor_tensor(out=dT[:, b, T_P:T], in0=s[:, S_AT + HIST:EXT], scalar=1.0 / w, in1=uE[:, b, S_AT + HIST:EXT],
                                             op0=ALU.mult, op1=ALU.subtract).then_inc(d_done, 1)
                for j in range(QKT):
                    n = TILES[j][1] if j < NT else KTILES[j - NT][1]
                    b, b0 = j % 2, 2 * (j % 2)
                    dve.wait_ge(qk_sq, QKT * l + j + 1)
                    if j >= 2:
                        dve.wait_ge(qk_T, QKT * l + j - 1)
                    if j < NT:
                        heads = sq[0:n, b, :].rearrange("p (h c) -> p h c", h=NH)
                        chain.step(dve.tensor_reduce(stat[0:n, b, 0:8], heads[:, :, 0:NOPE], AX.X, ALU.add))
                        dve.tensor_reduce(stat[0:n, b, 8:16], heads[:, :, NOPE:QK], AX.X, ALU.add).then_inc(qk_sum, 1)
                    else:
                        heads = sq[0:n, b, 0:512].rearrange("p (h c) -> p h c", h=NH)
                        chain.step(dve.memset(stat[0:n, b, 8:16], 1.0))
                        dve.tensor_reduce(stat[0:n, b, 0:8], heads, AX.X, ALU.add).then_inc(qk_sum, 1)
                    dve.wait_ge(qk_rms, QKT * l + j + 1)
                    chain.step(dve.reciprocal(rst[0:n, b, :], rst[0:n, b, :]))
                    chain.sync()
                    rows = tok[0:n, b, :].rearrange("p (h c) -> p h c", h=NH)
                    if j < NT:
                        for g in range(2):
                            src = PS[0:n, b0 + g, 0:384].rearrange("p (h c) -> p h c", h=4)
                            r = rst[0:n, b, 4 * g:4 * g + 4].unsqueeze(2)
                            chain.step(dve.tensor_tensor(rows[:, 4 * g:4 * g + 4, 0:NOPE], src[:, :, 0:NOPE], r.to_broadcast([n, 4, NOPE]), ALU.mult))
                            r = rst[0:n, b, 8 + 4 * g:12 + 4 * g].unsqueeze(2)
                            chain.step(dve.tensor_tensor(ropeX[0:n, 4 * g:4 * g + 4, :], src[:, :, NOPE:QK], r.to_broadcast([n, 4, ROPE]), ALU.mult))
                        chain.sync()
                        rotate(rows[:, :, NOPE:QK], ropeX[0:n], qtab, j, n, NH).then_inc(qk_norm, 1)
                    else:
                        r = rst[0:n, b, 0:8].unsqueeze(2).to_broadcast([n, NH, NOPE])
                        dve.tensor_tensor(rows[:, :, 0:NOPE], PS[0:n, b0, :].rearrange("p (h c) -> p h c", h=NH), r,
                                          ALU.mult).then_inc(qk_norm, 1)
                U = len(UNITS)

                def normalise(u):
                    i, h = UNITS[u]
                    at, n = TILES[i]
                    nk = at + P if i < 4 else PAST + T_S
                    dve.wait_ge(exp_done, U * l + u + 1)
                    b = u % 2
                    chain.step(dve.reciprocal(rinv[0:n, b:b + 1], psumr[0:n, b:b + 1]))
                    chain.sync()
                    dve.tensor_scalar(prob[0:n, b, 0:nk], prob[0:n, b, 0:nk], rinv[0:n, b:b + 1], None, ALU.mult).then_inc(p_done, 1)

                def heads_done(i):
                    at, n = TILES[i]
                    dve.wait_ge(pv_done, U * l + NH * (i + 1))
                    dve.tensor_copy(hT[:, 0:4, at:at + n], PS[:, 4 + i % 2, :].rearrange("p (b t) -> p b t", b=4)[:, :, 0:n]).then_inc(o_copied, 1)

                for u in range(U + 1):
                    if u < U:
                        i, h = UNITS[u]
                        at, n = TILES[i]
                        nk = at + P if i < 4 else PAST + T_S
                        dve.wait_ge(s_done, U * l + u + 1)
                        if i < 4:
                            chain.step(dve.memset(PS[0:CHUNK, u % 2, nk - CHUNK:nk], NEG))
                            chain.sync()
                        dve.tensor_reduce(nmax[0:n, u % 2:u % 2 + 1], PS[0:n, u % 2, 0:nk], AX.X, ALU.max, negate=True).then_inc(max_done, 1)
                    if u >= 1:
                        normalise(u - 1)
                    if u >= NH + 3 and (u - 3) % NH == 0:
                        heads_done((u - 3) // NH - 1)
                heads_done(NT - 1)
                for m in range(KD):
                    dve.wait_ge(y_done, KD * l + m + 1)
                    add_gated(2 * (m % 4), m, 16, x_done)

            def route():
                dve.wait_ge(lg_done, 1)
                dve.wait_ge(setup, 1)
                v = PS[:, 0, 0:NT * N_EXP].rearrange("p (t e) -> p t e", t=NT)
                brb = br[:].unsqueeze(1).to_broadcast([P, 4, N_EXP])
                chain.step(dve.tensor_tensor(logit[:, 0:4, :], v[:, 0:4, :], brb, ALU.add))
                chain.step(dve.tensor_tensor(logit[0:T_S, 4, :], v[0:T_S, 4, :], br[0:T_S, :], ALU.add))
                chain.sync()
                for t in range(NT):
                    chain.step(dve.max(top[:, t, :], logit[:, t, :]))
                chain.sync()
                for t in range(NT):
                    chain.step(dve.max_index(topi[:, t, :], top[:, t, :], logit[:, t, :]))
                chain.sync()
                chain.step(dve.tensor_copy(topf[:], topi[:]))
                dve.tensor_tensor(tw[:, :, 0:1], top[:, :, 1:2], top[:, :, 0:1], ALU.subtract).then_inc(tw_done, 1)
                dve.wait_ge(top_done, 1)
                chain.step(dve.tensor_scalar(tw[:, :, 2:3], tw[:, :, 1:2], 1.0, None, ALU.add))
                chain.sync()
                chain.step(dve.reciprocal(tw[:, :, 3:4], tw[:, :, 2:3]))
                chain.sync()
                chain.step(dve.tensor_tensor(tw[:, :, 2:3], tw[:, :, 1:2], tw[:, :, 3:4], ALU.mult))
                chain.sync()
                ids = iota8[:].unsqueeze(1).to_broadcast([P, NT, N_EXP])
                for k, (buf, w) in enumerate(((comb, 3), (comb2, 2))):
                    chain.step(dve.tensor_tensor(buf[:], topf[:, :, k:k + 1].to_broadcast([P, NT, N_EXP]), ids, ALU.is_equal))
                    chain.sync()
                    chain.step(dve.tensor_tensor(buf[:], buf[:], tw[:, :, w:w + 1].to_broadcast([P, NT, N_EXP]), ALU.mult))
                    chain.sync()
                dve.tensor_tensor(comb[:], comb[:], comb2[:], ALU.add).then_inc(comb_done, 1)

            def ffn(l):
                e0, ne = parts(l)
                if l == 1:
                    route()
                with dve.Fori(0, ne) as i:
                    e = i + e0
                    for c in range(KF):
                        b0 = 4 * (c % 2)
                        if l == 0:
                            dve.wait_ge(silu_done, e * KF + c + 1)
                        else:
                            dve.wait_ge(sgc_done, i * KF + c + 1)
                        dve.wait_ge(up_done, e * KF + c + 1)
                        dve.tensor_tensor(mid[:, c, :].rearrange("p (h t) -> p h t", h=2), sg[:, c % 2, :].rearrange("p (h t) -> p h t", h=2),
                                          PS[:, b0 + 2:b0 + 4, 0:HALF], ALU.mult).then_inc(mid_done, 1)
                    for m in range(KD):
                        dve.wait_ge(down_done, e * KD + m + 1)
                        add_gated(2 * (m % 4), m, 40, acc_done)

            dve.memset(ones[:], 1.0).then_inc(acc_done, 1)
            dve.memset(logit[:], 0.0)
            dve.memset(uE[:, :, 0:HIST], 0.0)
            dve.memset(eps[:], EPS).then_inc(setup, 1)
            dve.wait_ge(const_in, 16 * CONSTS)
            dve.memset(g96[NOPE:QK, :, :], 1.0).then_inc(gains_set, 1)
            dve.wait_ge(gains_set, 1)
            dve.tensor_scalar(g96[:, :, 0], g96[:, :, 0], SCALE, None, ALU.mult).then_inc(gains_set, 1)
            for l in range(DEPTH):
                modulation(l)
                norm(2 * l)
                mixer(l)
                norm(2 * l + 1)
                ffn(l)

        @block.gpsimd
        def _(pool):
            chain = Chain(pool, pool_chain)

            def tables(l):
                if l:
                    pool.wait_ge(qk_norm, QKT)
                hr = ROPE // 2
                for j, tab in enumerate((qtab, ktab)):
                    for half, lo, hi in ((0, 0, ROPE), (1, 0, hr), (1, hr, ROPE)):
                        ga, gb = (lo, hi) if half == 0 else (hr - lo, hr - lo + hr)
                        pool.tensor_tensor(tab[:, half, :, lo:hi], cs[:, half, :, lo:hi],
                                           grow[:, l, j, ga:gb].unsqueeze(1).to_broadcast([P, NT, hi - lo]), ALU.mult).then_inc(tab_done, 1)

            def norm(n):
                l, which = n // 2, n % 2
                pool.wait_ge(mod_done, 3 * (l + 1))
                for k in range(KD):
                    pool.wait_ge(hn_done, KD * n + k + 1)
                    pool.tensor_scalar(hT[:, k, T_P:T], hT[:, k, T_P:T], amod[:, which, k, 1:2], mod[:, 24 * which + k, 1:2],
                                       ALU.mult, ALU.add).then_inc(h_sample, 1)

            def windows(l):
                if l == 0:
                    pool.wait_ge(setup, 1)
                pool.wait_ge(past_in, 64 * (l + 1))
                for b in range(POOL_G):
                    pool.wait_ge(u_copied, 3 * (POOL_G * l + b + 1))
                    if b >= 1 or l:
                        pool.wait_ge(d_done, POOL_G * l + b)
                    src = uE[:, b, :]
                    for i in range(b + 1):
                        dst = win[:, (b + b - i) % 2, :]
                        step = 1 << i
                        lo = 2 * step - 1
                        chain.step(pool.tensor_tensor(dst[:, lo:EXT], src[:, lo:EXT], src[:, lo - step:EXT - step], ALU.add))
                        chain.sync()
                        src = dst
                    pool.tensor_tensor(src[:, HIST:HIST + 16], src[:, HIST:HIST + 16], ptab[:, b, :], ALU.mult).then_inc(win_done, 1)

            def rope_keys(l):
                for j in range(NKT):
                    n = KTILES[j][1]
                    jj = j + NT
                    pool.wait_ge(qk_T, QKT * l + jj - 1)
                    rows = tok[0:n, jj % 2, :].rearrange("p (h c) -> p h c", h=NH)
                    pool.tensor_copy(rows[:, :, NOPE:QK], kr[0:n, j:j + 1, :].to_broadcast([n, NH, ROPE])).then_inc(krc_done, 1)

            pool.wait_ge(const_in, 16 * CONSTS)
            for l in range(DEPTH):
                tables(l)
                norm(2 * l)
                windows(l)
                rope_keys(l)
                norm(2 * l + 1)
            n0 = chain.n
            pool.wait_ge(cr_copied, N_EXP)
            with pool.Fori(0, N_EXP) as i:
                pool.tensor_copy(rstd[:], combR[:, bass.ds(i, 1), :].rearrange("p a t -> p (a t)")).then_inc(pool_chain, 1)
                pool.wait_ge(pool_chain, i + n0 + 1)
                for c in range(KF):
                    pool.wait_ge(silu_done, (i + N_DENSE_PARTS) * KF + c + 1)
                    pool.tensor_tensor(sg[:, c % 2, :], sg[:, c % 2, :], rstd[:], ALU.mult).then_inc(sgc_done, 1)
                pool.wait_ge(sgc_done, (i + 1) * KF)


def constants():
    import numpy as np
    inv = (1.0 / (10000.0 ** (np.arange(0, ROPE, 2, dtype=np.float32) / np.float32(ROPE)))).astype(np.float32)
    pos = np.concatenate([np.arange(T_P), PAST + np.arange(T_S), np.zeros(NT * P - T)]).astype(np.float32)
    ang = (pos[:, None] * inv[None, :]).astype(np.float32).astype(np.float64)
    c, s = np.cos(ang), np.sin(ang)
    cs = np.stack([np.concatenate([c, c], 1), np.concatenate([-s, s], 1)]).astype(np.float32)
    cs = cs.reshape(2, NT, P, ROPE).transpose(2, 0, 1, 3)
    ptab = np.ones((P, POOL_G, 16), np.float32)
    for g in range(POOL_G):
        w = 2 << g
        ptab[:, g, :] = w / np.minimum(np.arange(16) + 1.0, w)
    iota8 = np.tile(np.arange(N_EXP, dtype=np.float32), (P, 1))
    return {"ident": np.eye(P, dtype=np.float32), "cs": np.ascontiguousarray(cs), "ptab": ptab, "iota8": iota8}


def kernel(**inp):
    import numpy as np
    import concourse.bacc as bacc
    from concourse.bass_utils import run_bass_kernel_spmd

    a = {k: np.asarray(v) for k, v in inp.items()}
    cols = lambda v: v.reshape(-1, v.shape[-1] // P, P)
    x = np.concatenate([a["x_prompt"][0], a["x_sample"][0]], 0)
    c = np.concatenate([a["c_prompt"], a["c_sample"]], 0)
    w_in = a["w_in"].reshape(DEPTH, KD, P, -1)
    w_lat = w_in[..., :LAT].transpose(0, 2, 1, 3)
    w_ukv = a["w_ukv"].reshape(DEPTH, KV_LORA, NH, NOPE + VD)
    w_ukv = np.concatenate([w_ukv[..., :NOPE].reshape(DEPTH, KV_LORA, -1), w_ukv[..., NOPE:].reshape(DEPTH, KV_LORA, -1)], -1)
    w_uq = a["w_uq"].reshape(DEPTH, 2, P, NH * QK).transpose(0, 2, 1, 3).reshape(DEPTH, P, -1)
    w_pool = a["w_pool"].transpose(0, 2, 1, 3).reshape(DEPTH, P, -1)

    def out_blocks(w, per):
        n, K, M = w.shape
        w = w.reshape(n, K // P, P, M // P // per, per, P)
        return w.transpose(0, 3, 2, 4, 1, 5).reshape(n, M // P // per, P, -1)

    def gate_up(g, u):
        g, u = out_blocks(g, 1), out_blocks(u, 1)
        return np.concatenate([g, u], -1)

    def split(w):
        return w[0].reshape(D, N_DENSE_PARTS, F_EXP).transpose(1, 0, 2)

    arrays = {
        "x": x.T.reshape(KD, P, T).transpose(1, 0, 2),
        "c": c.T.reshape(KD, P, 2).transpose(1, 0, 2),
        "ada": a["w_ada"].reshape(DEPTH, KD, P, ADA_N, ADA_W).transpose(0, 3, 2, 1, 4).reshape(DEPTH, ADA_N, P, -1),
        "b_ada": cols(a["b_ada"]).transpose(2, 0, 1),
        "g_norm": np.stack([cols(a["g_mix"]), cols(a["g_ffn"])], 1).transpose(3, 0, 1, 2),
        "g_lat": np.concatenate([cols(a["g_q_lat"]), cols(a["g_kv_lat"])], 1).transpose(2, 0, 1),
        "g_nope": np.stack([a["g_qn_nope"], a["g_kn_nope"]], -1),
        "g_rope": np.stack([a["g_qn_rope"], a["g_kn_rope"]], 1),
        "pool_scale": cols(a["pool_scale"]).transpose(2, 0, 1),
        "w_router": a["w_router"][0].reshape(KD, P, N_EXP).transpose(1, 0, 2),
        "b_router": a["b_router"][0],
        "krope": a["cache_krope"].reshape(DEPTH, 2, P, ROPE),
        "ckv": a["cache_ckv"][:, 0].transpose(0, 2, 1),
        "hist": a["state_pool"][:, 0].reshape(DEPTH, HIST, POOL_G, P).transpose(0, 3, 2, 1),
        "w_t0": w_lat[:, :, 0:4].reshape(DEPTH, P, -1),
        "w_t1": np.concatenate([w_lat[:, :, 4:8].reshape(DEPTH, P, -1), w_pool], -1),
        "w_u": out_blocks(a["w_in"][..., LAT:], 2),
        "w_q": np.concatenate([w_uq, w_ukv], -1),
        "w_o": out_blocks(a["w_out"], 2),
        "w_gu": gate_up(split(a["w_ffn_gate"]), split(a["w_ffn_up"])),
        "w_dn": out_blocks(a["w_ffn_down"][0].reshape(N_DENSE_PARTS, F_EXP, D), 2),
        "e_gu": gate_up(a["w_exp_gate"][0], a["w_exp_up"][0]),
        "e_dn": out_blocks(a["w_exp_down"][0], 2),
    }
    arrays.update(constants())
    arrays = {f"in_{k}": np.ascontiguousarray(v) for k, v in arrays.items()}
    outs = {"y": (P, KD, T), "ckv": (DEPTH, P, T), "krope": (DEPTH, P, NT, ROPE), "pool": (DEPTH, P, POOL_G, 2, HIST)}

    nc = bacc.Bacc("TRN2", target_bir_lowering=False, num_devices=1)
    d = {k[3:]: nc.dram_tensor(k, v.shape, mybir.dt.from_np(v.dtype), kind="ExternalInput").ap() for k, v in arrays.items()}
    o = {k: nc.dram_tensor(f"out_{k}", s, F32, kind="ExternalOutput").ap() for k, s in outs.items()}
    build(nc, d, o)
    r = run_bass_kernel_spmd(nc, [arrays], core_ids=[0]).results[0]
    y = r["out_y"].transpose(1, 0, 2).reshape(D, T).T
    ckv = r["out_ckv"].transpose(0, 2, 1)
    kr = r["out_krope"].transpose(0, 2, 1, 3).reshape(DEPTH, NT * P, ROPE)
    pool = r["out_pool"].transpose(3, 0, 4, 2, 1).reshape(2, DEPTH, HIST, POOL_G * P)
    C = np.ascontiguousarray
    return (C(y[None, :T_P]), C(y[None, T_P:]), C(ckv[:, None, :T_P]), C(kr[:, None, :T_P]), C(pool[0][:, None]),
            C(ckv[:, None, T_P:]), C(kr[:, None, T_P:T]), C(pool[1][:, None]))
```

```python
from contextlib import ExitStack

import concourse.bass as bass
from concourse import mybir

ALU = mybir.AluOpType
ACT = mybir.ActivationFunctionType
F32 = mybir.dt.float32
U32 = mybir.dt.uint32
F32R = mybir.dt.float32r
AX = mybir.AxisListType

P = 128
D = 1024
KD = D // P
T_P, T_S = 512, 64
T = T_P + T_S
HALF = T // 2
DEPTH = 2
PAST = 256
CHUNK = 64
NH = 8
Q_LORA, KV_LORA = 256, 128
NOPE, ROPE, VD = 64, 32, 64
QK = NOPE + ROPE
LAT = Q_LORA + KV_LORA + ROPE
POOL_G = 4
HIST = 15
N_EXP = 8
F_EXP = 1408
KF = F_EXP // P
W_GU = F_EXP // 4
W_DN = D // 4
GRP_T = 3
GRP = GRP_T * P
MAX_OVER = 2
N_LIST = N_EXP + MAX_OVER + 1
MOE_SLOTS = 4
GRP_CHUNKS = 12
UNITS_G = 2 * GRP_CHUNKS
UNIT_W = 6 * W_DN
DENSE_UNITS = 2 * KF + 2 * KD
N_DENSE_PARTS = 2
EPS = 1e-6
SCALE = QK ** -0.5
NEG = -1e30

TILES = [(t * P, min(P, T - t * P)) for t in range((T + P - 1) // P)]
KEYS = T_P + PAST + T_S
KTILES = [(t * P, min(P, KEYS - t * P)) for t in range((KEYS + P - 1) // P)]
NT, NKT = len(TILES), len(KTILES)
EXT = HIST + T_P + HIST + T_S
S_AT = HIST + T_P

SLOTS = 5
SLOT = 2 * KF * P
ADA_W = 256
ADA_N = 6 * D // ADA_W
MIX_N = 9
EXP_N = KF + KD // 2

UNITS = [(i, h) for i in range(NT) for h in range(NH)]


def layer_chunks(l):
    base = l * (ADA_N + MIX_N + N_DENSE_PARTS * EXP_N)
    return base, base + ADA_N, base + ADA_N + MIX_N


def build(nc, d, o):
    with ExitStack() as ctx:
        def sb(name, shape, dt=F32):
            return ctx.enter_context(nc.sbuf_tensor(name, shape, dt))

        def sem(name):
            return ctx.enter_context(nc.semaphore(name))

        PS = ctx.enter_context(nc.psum_tensor("PS", [P, 8, 512], F32))

        big = sb("big", [P, SLOTS * SLOT + KD * T])
        ring = big[:, 0:SLOTS * SLOT].rearrange("p (s n) -> p s n", s=SLOTS)
        x = sb("x", [P, KD, T])
        hT = big[:, SLOTS * SLOT:].rearrange("p (k t) -> p k t", k=KD)

        dT = hT[:, 4:8, :]
        stat = sb("stat", [P, 2, 16])
        rst = sb("rst", [P, 2, 16])
        nmax = sb("nmax", [P, 2])
        psumr = sb("psumr", [P, 2])
        rinv = sb("rinv", [P, 2])
        mod = sb("mod", [P, 48, 2])
        amod = sb("amod", [P, 2, KD, 2])
        ident = sb("ident", [P, P])
        ones = sb("ones", [P, P])
        eps = sb("eps", [P, 1])
        cs = sb("cs", [P, 2, NT, ROPE])
        ptab = sb("ptab", [P, POOL_G, 16])
        gmix = sb("gmix", [P, DEPTH, 2, KD])
        glat = sb("glat", [P, DEPTH, 3])
        g96 = sb("g96", [QK, DEPTH, 2])
        grow = sb("grow", [P, DEPTH, 2, ROPE])
        pscale = sb("pscale", [P, DEPTH, POOL_G])
        wr = sb("wr", [P, KD, N_EXP])
        br = sb("br", [P, N_EXP])
        logit = sb("logit", [P, NT, N_EXP])
        top = sb("top", [P, NT, 8])
        topi = sb("topi", [P, NT, 8], U32)
        topf = sb("topf", [P, NT, 8])
        iota8 = sb("iota8", [P, N_EXP])
        tw = sb("tw", [P, NT, 4])
        oh = sb("oh", [P, 2, NT, N_EXP])
        picked = sb("picked", [P, NT, N_EXP])
        rank = sb("rank", [P, NT + 1, N_EXP])
        over = sb("over", [P, 6, N_EXP])
        pos_e = sb("pos_e", [P, 2, NT, N_EXP])
        pos_f = sb("pos_f", [P, 2, NT])
        pos = sb("pos", [P, 2, NT], U32)
        lists = sb("lists", [N_LIST * GRP_T, P])
        slot_tok = sb("slot_tok", [P, N_LIST * GRP_T], U32)
        group_tok = sb("group_tok", [P, GRP_T], U32)
        tabf = sb("tabf", [P, 16])
        tab = sb("tab", [P, 16], U32)
        before = sb("before", [P, P])
        econst = sb("econst", [P, 3, N_EXP])
        tok_id = sb("tok_id", [P, NT])

        scT = sb("scT", [P, KD, 2])
        qtab = sb("qtab", [P, 2, NT, ROPE])
        ktab = sb("ktab", [P, 2, NT, ROPE])
        bada = sb("bada", [P, DEPTH, 48])
        zeros = sb("zeros", [P, D // 4])
        mixer_only = ctx.enter_context(ExitStack())
        def msb(name, shape, dt=F32):
            return mixer_only.enter_context(nc.sbuf_tensor(name, shape, dt))

        work = msb("work", [P, NH * (T + KEYS) + NKT * 512])
        qT = work[0:QK, 0:NH * T].rearrange("p (h t) -> p h t", h=NH)
        kT = work[0:QK, NH * T:NH * (T + KEYS)].rearrange("p (h t) -> p h t", h=NH)
        V = work[:, NH * (T + KEYS):].rearrange("p (t n) -> p t n", t=NKT)
        qlT = msb("qlT", [P, 2, T])
        ckvT = msb("ckvT", [P, KEYS])
        uE = msb("uE", [P, POOL_G, EXT])
        win = msb("win", [P, 2, EXT])
        rstd = msb("rstd", [P, T])
        tok = msb("tok", [P, 2, NH * QK])
        sq = msb("sq", [P, 2, NH * QK])
        ropeA = msb("ropeA", [P, NH, ROPE])
        ropeB = msb("ropeB", [P, NH, ROPE])
        ropeX = msb("ropeX", [P, NH, ROPE])
        kr = msb("kr", [P, NKT, ROPE])
        prob, probT = sq[:, :, 0:512], tok[:, :, 0:512]
        modrow = msb("modrow", [2, 5, ADA_W])
        cT = msb("cT", [P, KD, 2])

        mixer_only.close()
        dense_only = ctx.enter_context(ExitStack())

        def dsb(name, shape):
            return dense_only.enter_context(nc.sbuf_tensor(name, shape, F32R))

        h_hi, h_lo = dsb("h_hi", [P, KD, T]), dsb("h_lo", [P, KD, T])
        dw_hi, dw_lo = dsb("dw_hi", [P, 2, D]), dsb("dw_lo", [P, 2, D])
        mid_hi, mid_lo = dsb("mid_hi", [P, KF, T]), dsb("mid_lo", [P, KF, T])
        sg, mid = hT[:, 0:2, :], hT[:, 2:4, :]
        dense_only.close()
        w_hi = sb("w_hi", [P, 4, UNIT_W], F32R)
        w_lo = sb("w_lo", [P, 4, UNIT_W], F32R)
        hg_hi = sb("hg_hi", [P, KD, GRP], F32R)
        hg_lo = sb("hg_lo", [P, KD, GRP], F32R)
        mt_hi = sb("mt_hi", [P, KF, GRP], F32R)
        mt_lo = sb("mt_lo", [P, KF, GRP], F32R)
        rest = big[:, MOE_SLOTS * SLOT:]
        mg = rest[:, 0:GRP_T * F_EXP].rearrange("p (t n) -> p t n", t=GRP_T)
        yg = rest[:, 0:GRP_T * D].rearrange("p (t n) -> p t n", t=GRP_T)
        rows4 = rest[:, 0:4 * D].rearrange("p (t n) -> p t n", t=4)
        hg = rest[:, GRP_T * F_EXP:GRP_T * (F_EXP + D)].rearrange("p (t n) -> p t n", t=GRP_T)

        const_in, x_in = sem("const_in"), sem("x_in")
        past_in = sem("past_in")
        out_sem = sem("stored")
        slot_full = [sem(f"slot_full{i}") for i in range(SLOTS)]
        setup = sem("setup")
        gains_set = sem("gains_set")
        silu_c = sem("silu_c")
        ada_done, row_done, modT_done, mod_done = sem("ada_done"), sem("row_done"), sem("modT_done"), sem("mod_done")
        tab_done = sem("tab_done")
        squared, ssum_done, ms_done, rms_done, hn_done = sem("squared"), sem("ssum_done"), sem("ms_done"), sem("rms_done"), sem("hn_done")
        h_prompt, h_sample = sem("h_prompt"), sem("h_sample")
        z_done, z_stat, zn_done, lat_T, lat_done = sem("z_done"), sem("z_stat"), sem("zn_done"), sem("lat_T"), sem("lat_done")
        kr_done = sem("kr_done")
        u_done, u_copied, win_done, d_done, pool_done, pool_copied = (
            sem("u_done"), sem("u_copied"), sem("win_done"), sem("d_done"), sem("pool_done"), sem("pool_copied"))
        qk_done, qk_sq, qk_sum, qk_rms, qk_norm, krc_done, qk_T, qk_copied = (
            sem("qk_done"), sem("qk_sq"), sem("qk_sum"), sem("qk_rms"), sem("qk_norm"), sem("krc_done"), sem("qk_T"), sem("qk_copied"))
        v_copied = sem("v_copied")
        s_done, max_done, exp_done, p_done, pT_done, pT_copied, pv_done, o_copied = (
            sem("s_done"), sem("max_done"), sem("exp_done"), sem("p_done"), sem("pT_done"), sem("pT_copied"), sem("pv_done"), sem("o_copied"))
        y_done, x_done = sem("y_done"), sem("x_done")
        silu_done, mid_done, acc_done = (
            sem("silu_done"), sem("mid_done"), sem("acc_done"))
        h_split_hi, h_split_lo, dw_split_hi, dw_split_lo, mid_split_hi, mid_split_lo, dense_unit = (
            sem("h_split_hi"), sem("h_split_lo"), sem("dw_split_hi"), sem("dw_split_lo"), sem("mid_split_hi"), sem("mid_split_lo"),
            sem("dense_unit"))
        lg_done, top_done, tw_done, picked_done, rank_done, pos_done, tab_ready = (
            sem("lg_done"), sem("top_done"), sem("tw_done"), sem("picked_done"), sem("rank_done"), sem("pos_done"), sem("tab_ready"))
        rows_T, rows_copied, scattered, list_in, list_T, list_done = (
            sem("rows_T"), sem("rows_copied"), sem("scattered"), sem("list_in"), sem("list_T"), sem("list_done"))
        rows_stored = [sem("rows_stored0"), sem("rows_stored1")]
        zero_set, y_cleared = sem("zero_set"), sem("y_cleared")
        gathered, gtok_done, g_T, g_hi, g_lo = sem("gathered"), sem("gtok_done"), sem("g_T"), sem("g_hi"), sem("g_lo")
        hi_done, lo_done, unit_done = sem("hi_done"), sem("lo_done"), sem("unit_done")
        gsilu, gmid, m_T, m_hi, m_lo, y_copied, y_stored = (
            sem("gsilu"), sem("gmid"), sem("m_T"), sem("m_hi"), sem("m_lo"), sem("y_copied"), sem("y_stored"))
        back_in, summed, back_T, added = [sem("back_in0"), sem("back_in1")], sem("summed"), sem("back_T"), sem("added")
        act_chain, dve_chain, pool_chain = sem("act_chain"), sem("dve_chain"), sem("pool_chain")

        PARTS = N_DENSE_PARTS
        MOE_AT = layer_chunks(1)[2]
        fills = [len(range(s, MOE_AT, SLOTS)) for s in range(MOE_SLOTS)]
        row_dst = nc.dram_tensor("h_rows", (T, D), F32, kind="Internal").ap()
        y_dst = nc.dram_tensor("y_slots", ((N_LIST - 1) * GRP, D), F32, kind="Internal").ap()
        list_dst = nc.dram_tensor("slot_list", (N_LIST * GRP, 1), F32, kind="Internal").ap()

        UNIT = [(m, j) for m in range(8) for j in range(2)]
        UNIT += [(8, 0), (9, 0), (8, 1), (9, 1), (10, 0), (10, 1), (11, 0), (11, 1)]
        TURN_MID = {6: [0], 7: [1], 10: [2], 11: [3], 12: [4], 14: [5], 15: [6], 16: [7], 17: [8, 9], 18: [10]}
        TURN_ROWS = {19: 0, 21: 1, 22: 2}

        def units_to(m):
            return UNIT.index((m, 1)) + 1

        def split_before(m):
            return units_to(m - MOE_SLOTS) if m >= MOE_SLOTS else units_to(m - MOE_SLOTS + GRP_CHUNKS) - UNITS_G

        def dense_half(u):
            if u < 2 * KF:
                return u // 2, u % 2 * D, D
            m, j = (u - 2 * KF) // 2, u % 2
            return KF + m // 2, (m % 2) * KF * P + j * 6 * P, (KF - 6 if j else 6) * P

        def half(m, j):
            if m < 8:
                return j * 4 * W_GU, 4 * W_GU
            return j * 6 * W_DN, (6 - j) * W_DN

        QKT = NT + NKT
        CONSTS = 20
        block = ctx.enter_context(nc.Block())

        class Chain:
            def __init__(self, eng, s):
                self.eng, self.s, self.n = eng, s, 0

            def step(self, ins):
                ins.then_inc(self.s, 1)
                self.n += 1

            def sync(self):
                self.eng.wait_ge(self.s, self.n)

        @block.sync
        def _(sp):
            def ffn_release(e, c):
                return dw_split_lo, e * DENSE_UNITS + (2 * c + 2 if c < KF else 2 * KF + 4 * (c - KF) + 4)

            release = []
            for l in range(DEPTH):
                release += [(ada_done, ADA_N * l + j + 1) for j in range(ADA_N)]
                release += [(z_done, NT * (l + 1)), (pool_done, POOL_G * (l + 1))]
                release += [(u_done, POOL_G * l + 2 * j + 2) for j in range(2)]
                release += [(qk_done, QKT * (l + 1))]
                release += [(y_done, KD * l + 2 * j + 2) for j in range(4)]
                release += [ffn_release(i, c) for i in range(N_DENSE_PARTS) for c in range(EXP_N)] if l == 0 else []

            def fill(g, src, n, after=None):
                if after is None and g >= SLOTS:
                    after = release[g - SLOTS]
                if after is not None:
                    sp.wait_ge(*after)
                sp.dma_start(ring[:, g % SLOTS, 0:n], src).then_inc(slot_full[g % SLOTS], 16)

            sp.dma_start(cT[:], d["c"]).then_inc(const_in, 16)
            fill(0, d["ada"][0, 0], KD * ADA_W)
            sp.dma_start(x[:], d["x"]).then_inc(x_in, 16)
            for dst, src in ((ident, "ident"), (cs, "cs"), (ptab, "ptab"), (bada, "b_ada"), (gmix, "g_norm"),
                             (glat, "g_lat"), (pscale, "pool_scale"), (wr, "w_router"), (iota8, "iota8"),
                             (before, "before"), (econst, "econst"), (tok_id, "tok_id")):
                sp.dma_start(dst[:], d[src]).then_inc(const_in, 16)
            for l in range(DEPTH):
                sp.dma_start(g96[0:NOPE, l, :], d["g_nope"][l]).then_inc(const_in, 16)
                for j in range(2):
                    sp.dma_start(grow[:, l, j, :], d["g_rope"][l, j].partition_broadcast(P)).then_inc(const_in, 16)
            sp.dma_start(br[:], d["b_router"].partition_broadcast(P)).then_inc(const_in, 16)
            for j in range(2):
                sp.dma_start(kr[:, 4 + j, :], d["krope"][0, j]).then_inc(past_in, 16)
            sp.dma_start(ckvT[:, T_P:T_P + PAST], d["ckv"][0]).then_inc(past_in, 16)
            sp.dma_start(uE[:, :, S_AT:S_AT + HIST], d["hist"][0]).then_inc(past_in, 16)
            for l in range(DEPTH):
                g_ada, g_mix, g_ffn = layer_chunks(l)
                for j in range(1 if l == 0 else 0, 5):
                    fill(g_ada + j, d["ada"][l, j], KD * ADA_W)
                with sp.Fori(1, ADA_N // 5) as i:
                    for j in range(5):
                        fill(g_ada + j, d["ada"][l, bass.ds(i * 5 + j, 1)].rearrange("a p n -> p (a n)"),
                             KD * ADA_W, after=(ada_done, ADA_N * l + (i - 1) * 5 + j + 1))
                for j in range(ADA_N - ADA_N % 5, ADA_N):
                    fill(g_ada + j, d["ada"][l, j], KD * ADA_W)
                mix = [(d["w_t0"][l], 4 * LAT), (d["w_t1"][l], 4 * LAT + POOL_G * P)]
                mix += [(d["w_u"][l, j], 2 * D) for j in range(2)]
                mix += [(d["w_q"][l], 2 * NH * QK + 2 * 512)]
                mix += [(d["w_o"][l, j], 2 * D) for j in range(4)]
                for j, (src, n) in enumerate(mix):
                    fill(g_mix + j, src, n)
                    if l == 1 and j == 0:
                        sp.wait_ge(qk_copied, 2 * QKT)
                        sp.wait_ge(out_sem, 16 * 6)
                        for b in range(2):
                            sp.dma_start(kr[:, 4 + b, :], d["krope"][1, b]).then_inc(past_in, 16)
                        sp.dma_start(ckvT[:, T_P:T_P + PAST], d["ckv"][1]).then_inc(past_in, 16)
                        sp.wait_ge(d_done, 4)
                        sp.dma_start(uE[:, :, S_AT:S_AT + HIST], d["hist"][1]).then_inc(past_in, 16)
                    if j == 4:
                        sp.wait_ge(lat_done, NT * (l + 1))
                        sp.dma_start(o["ckv"][l, :, 0:T_P], ckvT[:, 0:T_P]).then_inc(out_sem, 16)
                        sp.dma_start(o["ckv"][l, :, T_P:T], ckvT[:, T_P + PAST:KEYS]).then_inc(out_sem, 16)
                        sp.wait_ge(kr_done, NT * (l + 1))
                        sp.dma_start(o["krope"][l, :, 0:4, :], kr[:, 0:4, :]).then_inc(out_sem, 16)
                        sp.dma_start(o["krope"][l, 0:T_S, 4, :], kr[0:T_S, NKT - 1, :]).then_inc(out_sem, 16)
                        sp.wait_ge(u_copied, POOL_G * 3 * (l + 1))
                        sp.dma_start(o["pool"][l, :, :, 0, :], uE[:, :, S_AT - HIST:S_AT]).then_inc(out_sem, 16)
                        sp.dma_start(o["pool"][l, :, :, 1, :], uE[:, :, EXT - HIST:EXT]).then_inc(out_sem, 16)
                if l == 1:
                    sp.wait_ge(zero_set, 2)
                    sp.dma_start(y_dst.rearrange("(p g) (h n) -> p (g h) n", p=P, h=4),
                                 zeros[:].unsqueeze(1).to_broadcast([P, 4 * (N_LIST - 1) * GRP_T, D // 4])).then_inc(y_cleared, 16)
                if l == 0:
                    width = lambda c: 2 * D if c < KF else SLOT
                    for c in range(EXP_N):
                        fill(g_ffn + c, d["w_gu"][0, c] if c < KF else d["w_dn"][0, c - KF], width(c))
                    with sp.Fori(1, N_DENSE_PARTS) as e:
                        for c in range(EXP_N):
                            src = d["w_gu"][bass.ds(e, 1), c] if c < KF else d["w_dn"][bass.ds(e, 1), c - KF]
                            fill(g_ffn + c, src.rearrange("a p n -> p (a n)"), width(c),
                                 after=ffn_release(e, c - SLOTS) if c >= SLOTS else ffn_release(e - 1, c - SLOTS + EXP_N))

            def expert_chunk(src, m, split):
                if split is not None:
                    sp.wait_ge(lo_done, split)
                sp.dma_start(ring[:, m % MOE_SLOTS, :], src).then_inc(slot_full[m % MOE_SLOTS], 16)

            for m in range(MOE_SLOTS):
                last = max(g for g in range(MOE_AT) if g % SLOTS == m)
                sp.wait_ge(*release[last])
                expert_chunk(d["e_w"][0, m], m, None)
            for t, (at, n) in enumerate(TILES):
                sp.wait_ge(rows_copied, t + 1)
                sp.dma_start(row_dst[at:at + n, :], rows4[0:n, t % 2, :]).then_inc(rows_stored[t % 2], 16)
            sp.wait_ge(scattered, 16 * 2 * NT)
            sp.dma_start(lists[:], list_dst.rearrange("(g p) o -> g (p o)", p=P)).then_inc(list_in, 16)
            for m in range(MOE_SLOTS, GRP_CHUNKS):
                expert_chunk(d["e_w"][0, m], m, split_before(m))
            with sp.Fori(1, N_EXP) as e:
                for m in range(GRP_CHUNKS):
                    expert_chunk(d["e_w"][bass.ds(e, 1), m].rearrange("a p n -> p (a n)"), m,
                                 e * UNITS_G + split_before(m))
            sp.wait_ge(tab_ready, 1)
            n_over = sp.value_load(tab[0:1, 12:13], min_val=0, max_val=MAX_OVER)
            for j in range(MAX_OVER):
                with sp.If(n_over > j):
                    e = sp.value_load(tab[0:1, 10 + j:11 + j], min_val=0, max_val=N_EXP - 1)
                    for m in range(GRP_CHUNKS):
                        expert_chunk(d["e_w"][bass.ds(e, 1), m].rearrange("a p n -> p (a n)"), m,
                                     (N_EXP + j) * UNITS_G + split_before(m))
            for m in range(2):
                expert_chunk(d["e_w"][0, m], m, n_over * UNITS_G + N_EXP * UNITS_G + split_before(m))
            sp.wait_ge(added, NT)
            sp.dma_start(o["y"], x[:]).then_inc(out_sem, 16)
            sp.wait_ge(out_sem, 16 * (6 * DEPTH + 1))

        @block.tensor
        def _(pe):
            def have(g, use=None):
                pe.wait_ge(slot_full[g % SLOTS], 16 * (g // SLOTS + 1) if use is None else (use + 1) * 16)

            def rms_sum(n):
                pe.wait_ge(ssum_done, n + 1)
                for h in range(2):
                    mm = pe.matmul(PS[:, 6 + h, 0:HALF], ones[:], rstd[:, h * HALF:(h + 1) * HALF], start=True, stop=True)
                mm.then_inc(ms_done, 1)

            def ada_chunk(l, j, jj, use, n, first):
                g = layer_chunks(l)[0] + jj
                have(g, use)
                if not first:
                    pe.wait_ge(row_done, n - 4)
                for k in range(KD):
                    mm = pe.matmul(PS[0:2, [0, 1, 3, 4, 5][jj % 5], 0:ADA_W], scT[:, k, :],
                                   ring[:, g % SLOTS, k * ADA_W:(k + 1) * ADA_W], start=(k == 0), stop=(k == KD - 1))
                mm.then_inc(ada_done, 1)

            def ada_turn(l, j, jj, n):
                pe.wait_ge(row_done, n + 1)
                for b in range(2):
                    at = j * 4 + b * 2
                    dst = PS[:, 2, at:at + 2] if isinstance(at, int) else PS[:, 2, bass.ds(at, 2)]
                    mm = pe.matmul(dst, modrow[:, jj % 5, b * P:(b + 1) * P], ident[0:2, 0:2],
                                   start=True, stop=True)
                mm.then_inc(modT_done, 1)

            def ada(l):
                n0 = l * ADA_N
                if l == 0:
                    pe.wait_ge(silu_c, 1)
                    pe.wait_ge(const_in, 16 * CONSTS)
                else:
                    pe.wait_ge(acc_done, KD * N_DENSE_PARTS + 1)
                base = layer_chunks(l)[0]

                def five(i, count, first):
                    for jj in range(count):
                        j = i * 5 + jj
                        ada_chunk(l, j, jj, None if isinstance(i, int) and False else i + (base + jj) // SLOTS, j + n0, first)
                    for jj in range(count):
                        ada_turn(l, i * 5 + jj, jj, i * 5 + jj + n0)
                five(0, 5, True)
                with pe.Fori(1, ADA_N // 5) as i:
                    five(i, 5, False)
                five(ADA_N // 5, ADA_N % 5, False)

            def mixer(l):
                g = layer_chunks(l)[1]
                pe.wait_ge(h_prompt, KD * (2 * l + 1))
                pe.wait_ge(h_sample, KD * (2 * l + 1))

                def latents(t):
                    at, n = TILES[t]
                    if t >= 2:
                        pe.wait_ge(kr_done, NT * l + t - 1)
                    for k in range(KD):
                        w = ring[:, (g + k // 4) % SLOTS, (k % 4) * LAT:(k % 4 + 1) * LAT]
                        if t == 0 and k % 4 == 0:
                            have(g + k // 4)
                        mm = pe.matmul(PS[0:n, t % 2, 0:LAT], hT[:, k, at:at + n], w, start=(k == 0), stop=(k == KD - 1))
                    mm.then_inc(z_done, 1)

                def latents_turn(t):
                    at, n = TILES[t]
                    pe.wait_ge(zn_done, NT * l + t + 1)
                    if t >= 2:
                        pe.wait_ge(lat_done, NT * l + t - 1)
                    for b in range(3):
                        mm = pe.transpose(PS[:, 2 + t % 2, b * P:b * P + n], tok[0:n, t % 2, b * P:(b + 1) * P], ident[0:n, 0:n])
                    mm.then_inc(lat_T, 1)

                for t in range(NT):
                    latents(t)
                    if t >= 1:
                        latents_turn(t - 1)
                latents_turn(NT - 1)
                for b in range(POOL_G):
                    s = (g + 2 + b // 2) % SLOTS
                    if b % 2 == 0:
                        have(g + 2 + b // 2)
                    if b >= 2:
                        pe.wait_ge(u_copied, 3 * (POOL_G * l + b - 1))
                    for h in range(2):
                        for k in range(KD):
                            mm = pe.matmul(PS[:, 4 + 2 * (b % 2) + h, 0:HALF], ring[:, s, (b % 2) * D + k * P:(b % 2) * D + (k + 1) * P],
                                           hT[:, k, h * HALF:(h + 1) * HALF], start=(k == 0), stop=(k == KD - 1))
                    mm.then_inc(u_done, 1)
                have(g + 4)
                wq = ring[:, (g + 4) % SLOTS, 0:2 * NH * QK].rearrange("p (k n) -> p k n", k=2)
                wk = ring[:, (g + 4) % SLOTS, 2 * NH * QK:2 * NH * QK + 1024]
                pe.wait_ge(lat_done, NT * (l + 1))
                pe.wait_ge(kr_done, NT * (l + 1))
                pe.wait_ge(past_in, 64 * (l + 1))

                def project(j):
                    b0 = 2 * (j % 2)
                    if j >= 2:
                        pe.wait_ge(qk_norm, QKT * l + j - 1)
                        if j >= NT + 2:
                            pe.wait_ge(v_copied, NKT * l + j - NT - 1)
                    if j < NT:
                        at, n = TILES[j]
                        for h in range(2):
                            for k in range(2):
                                mm = pe.matmul(PS[0:n, b0 + h, 0:384], qlT[:, k, at:at + n], wq[:, k, h * 384:(h + 1) * 384],
                                               start=(k == 0), stop=(k == 1))
                    else:
                        at, n = KTILES[j - NT]
                        for h in range(2):
                            mm = pe.matmul(PS[0:n, b0 + h, :], ckvT[:, at:at + n], wk[:, h * 512:(h + 1) * 512], start=True, stop=True)
                    mm.then_inc(qk_done, 1)

                def heads_turn(j):
                    at, n = TILES[j] if j < NT else KTILES[j - NT]
                    pe.wait_ge(qk_norm, QKT * l + j + 1)
                    if j >= NT:
                        pe.wait_ge(krc_done, NKT * l + j - NT + 1)
                    if j >= 2:
                        pe.wait_ge(qk_copied, 2 * (QKT * l + j - 1))
                    else:
                        pe.wait_ge(u_copied, 3 * POOL_G * (l + 1))
                    for h in range(NH):
                        mm = pe.transpose(PS[0:QK, 4 + 2 * (j % 2) + h // 4, (h % 4) * P:(h % 4) * P + n],
                                          tok[0:n, j % 2, h * QK:(h + 1) * QK], ident[0:n, 0:n])
                    mm.then_inc(qk_T, 1)

                for j in range(QKT):
                    project(j)
                    if j >= 1:
                        heads_turn(j - 1)
                heads_turn(QKT - 1)
                pe.wait_ge(qk_copied, 2 * QKT * (l + 1))
                for b in range(POOL_G):
                    pe.wait_ge(d_done, POOL_G * l + b + 1)
                    if b >= 2:
                        pe.wait_ge(pool_copied, POOL_G * l + b - 1)
                    for h in range(2):
                        mm = pe.matmul(PS[:, 4 + 2 * (b % 2) + h, 0:HALF], ring[:, (g + 1) % SLOTS, 4 * LAT + b * P:4 * LAT + (b + 1) * P],
                                       dT[:, b, h * HALF:(h + 1) * HALF], start=True, stop=True)
                    mm.then_inc(pool_done, 1)
                pe.wait_ge(pool_copied, POOL_G * (l + 1))
                U = len(UNITS)

                def scores(u):
                    i, h = UNITS[u]
                    at, n = TILES[i]
                    k0, nk = (0, at + P) if i < 4 else (T_P, PAST + T_S)
                    if u >= 2:
                        pe.wait_ge(exp_done, U * l + u - 1)
                    else:
                        pe.wait_ge(v_copied, NKT * (l + 1))
                    pe.matmul(PS[0:n, u % 2, 0:nk], qT[:, h, at:at + n], kT[:, h, k0:k0 + nk], start=True, stop=True).then_inc(s_done, 1)

                def key_blocks(i):
                    return [(b, b, P) for b in range(i + 1)] if i < 4 else [(b, 4 + b, KTILES[4 + b][1]) for b in range(3)]

                def probs_turn(u):
                    i, h = UNITS[u]
                    n = TILES[i][1]
                    pe.wait_ge(p_done, U * l + u + 1)
                    if u >= 2:
                        pe.wait_ge(pT_copied, U * l + u - 1)
                    for b, kb, nk in key_blocks(i):
                        mm = pe.transpose(PS[0:nk, 2 + u % 2, b * P:b * P + n], prob[0:n, u % 2, b * P:b * P + nk], ident[0:n, 0:n])
                    mm.then_inc(pT_done, 1)

                def values(u):
                    i, h = UNITS[u]
                    n = TILES[i][1]
                    pe.wait_ge(pT_copied, U * l + u + 1)
                    if h == 0 and i >= 2:
                        pe.wait_ge(o_copied, NT * l + i - 1)
                    r = (h % 2) * VD
                    kb_ = key_blocks(i)
                    for m, (b, kb, nk) in enumerate(kb_):
                        mm = pe.matmul(PS[r:r + VD, 4 + i % 2, (h // 2) * P:(h // 2) * P + n], V[0:nk, kb, h * VD:(h + 1) * VD],
                                       probT[0:nk, u % 2, b * P:b * P + n], start=(m == 0), stop=(m == len(kb_) - 1))
                    mm.then_inc(pv_done, 1)

                for u in range(U + 2):
                    if u < U:
                        scores(u)
                    if 1 <= u <= U:
                        probs_turn(u - 1)
                    if u >= 2:
                        values(u - 2)
                pe.wait_ge(o_copied, NT * (l + 1))
                for m in range(KD):
                    s = (g + 5 + m // 2) % SLOTS
                    if m % 2 == 0:
                        have(g + 5 + m // 2)
                    if m >= 4:
                        pe.wait_ge(x_done, KD * l + m - 3)
                    for h in range(2):
                        for k in range(KD):
                            mm = pe.matmul(PS[:, 2 * (m % 4) + h, 0:HALF], ring[:, s, (m % 2) * D + k * P:(m % 2) * D + (k + 1) * P],
                                           hT[:, k, h * HALF:(h + 1) * HALF], start=(k == 0), stop=(k == KD - 1))
                    mm.then_inc(y_done, 1)

            def ffn(l):
                with pe.Fori(0, N_DENSE_PARTS) as e:
                    for u in range(DENSE_UNITS):
                        pe.wait_ge(dw_split_lo, e * DENSE_UNITS + u + 1)
                        if u < 2 * KF:
                            c, w = u // 2, u % 2
                            if w == 0:
                                pe.wait_ge(*((mid_done, e * KF + c - 1) if c >= 2 else (acc_done, e * KD + 1)))
                            bank, ks, n, a_hi, a_lo = 4 * (c % 2) + 2 * w, range(KD), KD, h_hi, h_lo
                        else:
                            m, j = (u - 2 * KF) // 2, u % 2
                            if j == 0:
                                if m == 0:
                                    pe.wait_ge(silu_done, e * KF + KF)
                                elif m == 1:
                                    pe.wait_ge(mid_done, e * KF + KF)
                                elif m >= 4:
                                    pe.wait_ge(acc_done, e * KD + m - 3 + 1)
                            if m == 0:
                                pe.wait_ge(mid_split_lo, e * KF + (6 if j == 0 else KF))
                            bank, ks, n, a_hi, a_lo = 2 * (m % 4), (range(6, KF) if j else range(6)), KF, mid_hi, mid_lo
                        for h in range(2):
                            for q, k in enumerate(ks):
                                if u == 0 and h == 0:
                                    pe.wait_ge(h_split_lo, k + 1)
                                W_hi, W_lo = dw_hi[:, u % 2, q * P:(q + 1) * P], dw_lo[:, u % 2, q * P:(q + 1) * P]
                                hi, lo = a_hi[:, k, h * HALF:(h + 1) * HALF], a_lo[:, k, h * HALF:(h + 1) * HALF]
                                for t, (w_, x_) in enumerate(((W_hi, hi), (W_hi, lo), (W_lo, hi))):
                                    mm = pe.matmul(PS[:, bank + h, 0:HALF], w_, x_, start=(k == 0 and t == 0), stop=(k == n - 1 and t == 2))
                        mm.then_inc(dense_unit, 1)

            def turn_rows():
                pe.wait_ge(h_prompt, KD * (2 * DEPTH))
                pe.wait_ge(h_sample, KD * (2 * DEPTH))
                for t, (at, n) in enumerate(TILES):
                    for k in range(KD):
                        mm = pe.matmul(PS[0:n, 0, t * N_EXP:(t + 1) * N_EXP], hT[:, k, at:at + n], wr[:, k, :],
                                       start=(k == 0), stop=(k == KD - 1))
                mm.then_inc(lg_done, 1)
                for t, (at, n) in enumerate(TILES):
                    if t >= 2:
                        pe.wait_ge(rows_copied, t - 1)
                    for k in range(KD):
                        mm = pe.transpose(PS[0:n, 2 + 2 * (t % 2) + k // 4, (k % 4) * P:(k % 4 + 1) * P], hT[:, k, at:at + n], ident[:])
                    mm.then_inc(rows_T, 1)
                pe.wait_ge(picked_done, 1)
                for t in range(NT):
                    cols = PS[:, 1, t * N_EXP:(t + 1) * N_EXP]
                    mm = pe.matmul(cols, before[:], picked[:, t, :], start=True, stop=(t == 0))
                    for q in range(t):
                        mm = pe.matmul(cols, ones[:], picked[:, q, :], start=False, stop=(q == t - 1))
                for t in range(NT):
                    mm = pe.matmul(PS[:, 1, NT * N_EXP:(NT + 1) * N_EXP], ones[:], picked[:, t, :], start=(t == 0), stop=(t == NT - 1))
                mm.then_inc(rank_done, 1)
                pe.wait_ge(list_in, 16)
                nl = N_LIST * GRP_T
                pe.transpose(PS[:, 1, 128:128 + nl], lists[:], ident[0:nl, 0:nl]).then_inc(list_T, 1)

            def turn_group(i, t):
                pe.wait_ge(gathered, (i + 1) * 16 * GRP_T)
                if t or not isinstance(i, int):
                    pe.wait_ge(g_lo, i * GRP_T + t)
                for k in range(KD):
                    mm = pe.transpose(PS[:, 6 + k // 4, (k % 4) * P:(k % 4 + 1) * P], hg[:, t, k * P:(k + 1) * P], ident[:])
                mm.then_inc(g_T, 1)

            def group(i):
                n = pe.value_load(tab[0:1, bass.ds(i, 1)], min_val=1, max_val=GRP_T)
                bank = lambda m, t: 3 * (m % 2) + t

                def tiles(body):
                    for t in range(GRP_T - 1, 0, -1):
                        with pe.If(n > t):
                            body(t)
                    return body(0)

                def turn_mid(f):
                    c = ((f + 1) * P - 1) // W_GU
                    pe.wait_ge(gmid, i * 4 + c + 1)
                    if f >= 2:
                        pe.wait_ge(m_lo, i * KF + f - 1)
                    elif f == 0:
                        pe.wait_ge(g_lo, (i + 1) * GRP_T)
                    tiles(lambda t: pe.transpose(PS[:, 6 + f % 2, t * P:(t + 1) * P], mg[:, t, f * P:(f + 1) * P], ident[:])).then_inc(m_T, 1)

                for u, (m, j) in enumerate(UNIT):
                        for f in TURN_MID.get(u, ()):
                            turn_mid(f)
                        if u == UNIT.index((8, 1)):
                            pe.wait_ge(m_lo, i * KF + KF)
                        if u in TURN_ROWS:
                            turn_group(i + 1, TURN_ROWS[u])
                        pe.wait_ge(lo_done, i * UNITS_G + u + 1)
                        b, w = u % 4, W_GU if m < 8 else W_DN
                        if m < 8:
                            if j == 0:
                                c = m // 2
                                if m == 0:
                                    pe.wait_ge(g_lo, (i + 1) * GRP_T)
                                if c:
                                    pe.wait_ge(gmid if m % 2 else gsilu, i * 4 + c)
                                else:
                                    pe.wait_ge(y_copied, i * 4 + 3 + m % 2)
                            ks, a_hi, a_lo = range(4 * j, 4 * j + 4), hg_hi, hg_lo
                            first, last = 0, KD - 1
                        else:
                            if j == 0:
                                if m == 8:
                                    pe.wait_ge(gsilu, i * 4 + 4)
                                    pe.wait_ge(m_lo, i * KF + 6)
                                elif m > 9:
                                    pe.wait_ge(y_copied, i * 4 + m - 5)
                            if m == 9 and j == 0:
                                pe.wait_ge(gmid, i * 4 + 4)
                            ks, a_hi, a_lo = range(6 * j, 6 if j == 0 else KF), mt_hi, mt_lo
                            first, last = 0, KF - 1

                        def body(t):
                            for q, k in enumerate(ks):
                                hi, lo = a_hi[:, k, t * P:(t + 1) * P], a_lo[:, k, t * P:(t + 1) * P]
                                W_hi, W_lo = w_hi[:, b, q * w:(q + 1) * w], w_lo[:, b, q * w:(q + 1) * w]
                                for r, (x_, w_) in enumerate(((hi, W_hi), (hi, W_lo), (lo, W_hi))):
                                    mm = pe.matmul(PS[:, bank(m, t), 0:w], x_, w_, start=(k == first and r == 0), stop=(k == last and r == 2))
                            return mm
                        tiles(body).then_inc(unit_done, 1)

            def experts():
                turn_rows()
                for t in range(GRP_T):
                    turn_group(0, t)
                pe.wait_ge(tab_ready, 1)
                with pe.Fori(0, pe.value_load(tab[0:1, 13:14], min_val=N_EXP, max_val=N_EXP + MAX_OVER)) as i:
                    group(i)
                for t, (at, n) in enumerate(TILES):
                    pe.wait_ge(summed, t + 1)
                    if t >= 2:
                        pe.wait_ge(added, t - 1)
                    for k in range(KD):
                        mm = pe.transpose(PS[:, 2 * (t % 2) + k // 4, (k % 4) * P:(k % 4) * P + n], rows4[0:n, 2 * (t % 2), k * P:(k + 1) * P],
                                          ident[0:n, 0:n])
                    mm.then_inc(back_T, 1)

            for l in range(DEPTH):
                ada(l)
                rms_sum(2 * l)
                mixer(l)
                rms_sum(2 * l + 1)
                if l == 0:
                    ffn(l)
                else:
                    experts()

        @block.scalar
        def _(act):
            chain = Chain(act, act_chain)

            def norm(n):
                l, which = n // 2, n % 2
                if n == 0:
                    act.wait_ge(x_in, 16)
                    act.wait_ge(setup, 1)
                elif which == 1:
                    act.wait_ge(x_done, KD * (l + 1))
                else:
                    act.wait_ge(acc_done, KD * N_DENSE_PARTS + 1)
                act.activation(hT, x[:], ACT.Square).then_inc(squared, 1)
                act.wait_ge(ms_done, n + 1)
                act.activation(rstd[:].rearrange("p (h t) -> p h t", h=2), PS[:, 6:8, 0:HALF], ACT.Sqrt,
                               bias=eps[:], scale=1.0 / D).then_inc(rms_done, 1)
                act.wait_ge(mod_done, 3 * (l + 1))
                for k in range(KD):
                    act.wait_ge(hn_done, KD * n + k + 1)
                    act.activation(hT[:, k, 0:T_P], hT[:, k, 0:T_P], ACT.Identity, bias=mod[:, 24 * which + k, 0:1],
                                   scale=amod[:, which, k, 0:1]).then_inc(h_prompt, 1)

            def ada(l):
                def copy(j, jj, n, first):
                    act.wait_ge(ada_done, n + 1)
                    if not first:
                        act.wait_ge(modT_done, n - 4)
                    act.copy(modrow[:, jj % 5, :], PS[0:2, [0, 1, 3, 4, 5][jj % 5], 0:ADA_W]).then_inc(row_done, 1)
                n0 = l * ADA_N
                for jj in range(5):
                    copy(jj, jj, n0 + jj, l == 0)
                with act.Fori(1, ADA_N // 5) as i:
                    for jj in range(5):
                        copy(i * 5 + jj, jj, i * 5 + jj + n0, False)
                for j in range(ADA_N - ADA_N % 5, ADA_N):
                    copy(j, j, n0 + j, False)

            def mixer(l):
                for t, (at, n) in enumerate(TILES):
                    act.wait_ge(z_done, NT * l + t + 1)
                    if t >= 2 or l > 0:
                        act.wait_ge(kr_done, NT * l + t - 1)
                    b = t % 2
                    for j, (c0, w) in enumerate(((0, Q_LORA), (Q_LORA, KV_LORA), (Q_LORA + KV_LORA, ROPE))):
                        chain.step(act.activation(sq[0:n, b, c0:c0 + w], PS[0:n, b, c0:c0 + w], ACT.Square,
                                                  scale=float(w) ** -0.5, accum_out=stat[0:n, b, j:j + 1]))
                    chain.sync()
                    act.activation(rst[0:n, b, 0:3], stat[0:n, b, 0:3], ACT.Sqrt, bias=eps[0:n, :]).then_inc(z_stat, 1)
                    if t >= 1:
                        latents_out(l, t - 1)
                latents_out(l, NT - 1)
                for b in range(POOL_G):
                    act.wait_ge(u_done, POOL_G * l + b + 1)
                    if b == 0:
                        act.wait_ge(win_done, POOL_G * l) if l else None
                        act.wait_ge(d_done, POOL_G * l) if l else None
                        act.wait_ge(out_sem, 16 * 6 * l) if l else None
                    b0 = 4 + 2 * (b % 2)
                    act.copy(uE[:, b, HIST:HIST + HALF], PS[:, b0, 0:HALF]).then_inc(u_copied, 1)
                    act.copy(uE[:, b, HIST + HALF:HIST + T_P], PS[:, b0 + 1, 0:T_P - HALF]).then_inc(u_copied, 1)
                    act.copy(uE[:, b, S_AT + HIST:EXT], PS[:, b0 + 1, T_P - HALF:HALF]).then_inc(u_copied, 1)
                for j in range(QKT):
                    n = TILES[j][1] if j < NT else KTILES[j - NT][1]
                    b0 = 2 * (j % 2)
                    act.wait_ge(qk_done, QKT * l + j + 1)
                    if j >= 2:
                        act.wait_ge(qk_sum, QKT * l + j - 1)
                    if j < NT:
                        act.activation(sq[0:n, j % 2, :].rearrange("p (h n) -> p h n", h=2), PS[0:n, b0:b0 + 2, 0:384],
                                       ACT.Square).then_inc(qk_sq, 1)
                    else:
                        act.activation(sq[0:n, j % 2, 0:512], PS[0:n, b0, :], ACT.Square).then_inc(qk_sq, 1)
                        act.copy(V[0:n, j - NT, :], PS[0:n, b0 + 1, :]).then_inc(v_copied, 1)
                    act.wait_ge(qk_sum, QKT * l + j + 1)
                    chain.step(act.activation(rst[0:n, j % 2, 0:8], stat[0:n, j % 2, 0:8], ACT.Sqrt, bias=eps[0:n, :], scale=1.0 / NOPE))
                    act.activation(rst[0:n, j % 2, 8:16], stat[0:n, j % 2, 8:16], ACT.Sqrt, bias=eps[0:n, :],
                                   scale=1.0 / ROPE).then_inc(qk_rms, 1)
                    if j >= 1:
                        heads_out(l, j - 1)
                heads_out(l, QKT - 1)
                for b in range(POOL_G):
                    act.wait_ge(pool_done, POOL_G * l + b + 1)
                    b0 = 4 + 2 * (b % 2)
                    act.activation(hT[:, 4 + b, :].rearrange("p (h t) -> p h t", h=2), PS[:, b0:b0 + 2, 0:HALF], ACT.Copy,
                                   scale=pscale[:, l, b:b + 1]).then_inc(pool_copied, 1)
                U = len(UNITS)

                def copy_probs(u):
                    i, h = UNITS[u]
                    n = TILES[i][1]
                    act.wait_ge(pT_done, U * l + u + 1)
                    if u >= 2:
                        act.wait_ge(pv_done, U * l + u - 1)
                    if i < 4:
                        w = (i + 1) * P
                        act.copy(probT[:, u % 2, 0:w], PS[:, 2 + u % 2, 0:w]).then_inc(pT_copied, 1)
                    else:
                        v = lambda b, n_, lo, hi: b[0:n_, lo * P:hi * P].rearrange("p (b t) -> p b t", t=P)[:, :, 0:n]
                        chain.step(act.copy(v(probT[:, u % 2, :], P, 0, 2), v(PS[:, 2 + u % 2, :], P, 0, 2)))
                        act.copy(v(probT[:, u % 2, :], T_S, 2, 3), v(PS[:, 2 + u % 2, :], T_S, 2, 3)).then_inc(pT_copied, 1)

                for u in range(U + 1):
                    if u < U:
                        i, h = UNITS[u]
                        at, n = TILES[i]
                        nk = at + P if i < 4 else PAST + T_S
                        act.wait_ge(max_done, U * l + u + 1)
                        if u >= 2:
                            act.wait_ge(pT_done, U * l + u - 1)
                        act.activation(prob[0:n, u % 2, 0:nk], PS[0:n, u % 2, 0:nk], ACT.Exp, bias=nmax[0:n, u % 2:u % 2 + 1],
                                       accum_out=psumr[0:n, u % 2:u % 2 + 1]).then_inc(exp_done, 1)
                    if u >= 1:
                        copy_probs(u - 1)

            def latents_out(l, t):
                at, n = TILES[t]
                kat = at if t < 4 else T_P + PAST
                act.wait_ge(lat_T, NT * l + t + 1)
                for b in range(2):
                    chain.step(act.activation(qlT[:, b, at:at + n], PS[:, 2 + t % 2, b * P:b * P + n], ACT.Copy, scale=glat[:, l, b:b + 1]))
                if l == 1 and t == 0:
                    act.wait_ge(out_sem, 16 * 6)
                act.activation(ckvT[:, kat:kat + n], PS[:, 2 + t % 2, 2 * P:2 * P + n], ACT.Copy, scale=glat[:, l, 2:3]).then_inc(lat_done, 1)

            def heads_out(l, j):
                at, n = TILES[j] if j < NT else KTILES[j - NT]
                act.wait_ge(qk_T, QKT * l + j + 1)
                dst = (qT if j < NT else kT)[:, :, at:at + n]
                for h in range(2):
                    src = PS[0:QK, 4 + 2 * (j % 2) + h, :].rearrange("p (b t) -> p b t", b=4)[:, :, 0:n]
                    act.activation(dst[:, 4 * h:4 * h + 4, :], src, ACT.Copy,
                                   scale=g96[:, l, (0 if j < NT else 1):(1 if j < NT else 2)]).then_inc(qk_copied, 1)

            def ffn(l):
                g = layer_chunks(l)[2]
                act.wait_ge(h_prompt, KD * (2 * l + 2))
                for k in range(KD):
                    act.wait_ge(h_sample, KD * (2 * l + 1) + k + 1)
                    act.copy(h_hi[:, k, :], hT[:, k, :]).then_inc(h_split_hi, 1)
                act.wait_ge(out_sem, 16 * 6)
                with act.Fori(0, N_DENSE_PARTS) as e:
                    def split(u):
                        c, a, w = dense_half(u)
                        act.wait_ge(slot_full[(g + c) % SLOTS], (e * (EXP_N // SLOTS) + (g + c) // SLOTS + 1) * 16)
                        act.wait_ge(dense_unit, e * DENSE_UNITS + u + 1)
                        act.copy(dw_hi[:, u % 2, 0:w], ring[:, (g + c) % SLOTS, a:a + w]).then_inc(dw_split_hi, 1)

                    split(0)
                    for u in range(DENSE_UNITS):
                        if u + 1 < DENSE_UNITS:
                            split(u + 1)
                        if u < 2 * KF and u % 2 == 1:
                            c, b0 = u // 2, 4 * (u // 2 % 2)
                            act.wait_ge(dense_unit, e * DENSE_UNITS + 2 * c + 3)
                            if c >= 2:
                                act.wait_ge(mid_done, e * KF + c - 1)
                            act.activation(sg[:, c % 2, :].rearrange("p (h t) -> p h t", h=2), PS[:, b0:b0 + 2, 0:HALF],
                                           ACT.Silu).then_inc(silu_done, 1)
                        if 2 <= u <= 2 * KF and u % 2 == 0:
                            c = u // 2 - 1
                            act.wait_ge(mid_done, e * KF + c + 1)
                            act.copy(mid_hi[:, c, :], mid[:, c % 2, :]).then_inc(mid_split_hi, 1)

            def split_unit(s, u):
                m, j = UNIT[u % UNITS_G]
                a, w = half(m, j)
                if j == 0:
                    k, sl = m + u // UNITS_G * GRP_CHUNKS, m % MOE_SLOTS
                    if isinstance(s, int):
                        act.wait_ge(slot_full[sl], 16 * (fills[sl] + k // MOE_SLOTS + 1))
                    else:
                        act.wait_ge(slot_full[sl], (s * (GRP_CHUNKS // MOE_SLOTS) + fills[sl] + k // MOE_SLOTS + 1) * 16)
                if not isinstance(s, int) and u > 3:
                    act.wait_ge(unit_done, s * UNITS_G + u - 3)
                act.copy(w_hi[:, u % 4, 0:w], ring[:, m % MOE_SLOTS, a:a + w]).then_inc(hi_done, 1)

            def turned_group(i, t):
                act.wait_ge(g_T, i * GRP_T + t + 1)
                act.copy(hg_hi[:, :, t * P:(t + 1) * P], PS[:, 6:8, :].rearrange("p b (k t) -> p (b k) t", k=4)).then_inc(g_hi, 1)

            def group(i):
                n = act.value_load(tab[0:1, bass.ds(i, 1)], min_val=1, max_val=GRP_T)

                def wide(op, s, *after):
                    with act.If(n > 1):
                        for a in after:
                            act.wait_ge(*a)
                        op(GRP_T).then_inc(s, 1)
                    with act.Else():
                        for a in after:
                            act.wait_ge(*a)
                        op(1).then_inc(s, 1)

                def turned_mid(u):
                    for f in TURN_MID.get(u, ()):
                        wide(lambda q: act.copy(mt_hi[:, f, 0:q * P], PS[:, 6 + f % 2, 0:q * P]), m_hi, (m_T, i * KF + f + 1))

                for u in range(UNITS_G):
                    if u in (17, 18):
                        turned_mid(u)
                    split_unit(i, u + 3)
                    if u < 16 and u % 4 == 2:
                        c = u // 4
                        left = [(y_stored, (i + 1) * 16)] if c == 0 else []
                        wide(lambda q: act.activation(mg[:, 0:q, c * W_GU:(c + 1) * W_GU], PS[:, 0:q, 0:W_GU], ACT.Silu),
                             gsilu, *left, (unit_done, i * UNITS_G + u))
                    if u < 17:
                        turned_mid(u)
                    if u in TURN_ROWS:
                        turned_group(i + 1, TURN_ROWS[u])
                    if u >= 16 and UNIT[u][1] == 1:
                        d_ = UNIT[u][0] - 8
                        wide(lambda q: act.copy(yg[:, 0:q, d_ * W_DN:(d_ + 1) * W_DN], PS[:, 3 * (d_ % 2):3 * (d_ % 2) + q, 0:W_DN]),
                             y_copied, (unit_done, i * UNITS_G + u + 1))

            def experts():
                for u in range(3):
                    split_unit(0, u)
                for t, (at, n) in enumerate(TILES):
                    act.wait_ge(rows_T, t + 1)
                    if t >= 2:
                        act.wait_ge(rows_stored[t % 2], 16 * (t // 2))
                    b0 = 2 + 2 * (t % 2)
                    act.copy(rows4[0:n, t % 2, :].rearrange("p (b n) -> p b n", b=2), PS[0:n, b0:b0 + 2, :]).then_inc(rows_copied, 1)
                    if t == 2:
                        act.wait_ge(tw_done, 1)
                        act.activation(tw[:, :, 1:2], tw[:, :, 0:1], ACT.Exp).then_inc(top_done, 1)
                for t in range(GRP_T):
                    turned_group(0, t)
                act.wait_ge(tab_ready, 1)
                with act.Fori(0, act.value_load(tab[0:1, 13:14], min_val=N_EXP, max_val=N_EXP + MAX_OVER)) as i:
                    group(i)

            act.wait_ge(const_in, 16 * CONSTS)
            act.activation(scT[:], cT[:], ACT.Silu).then_inc(silu_c, 1)
            act.wait_ge(gains_set, 2)
            for l in range(DEPTH):
                ada(l)
                norm(2 * l)
                mixer(l)
                norm(2 * l + 1)
                ffn(l) if l == 0 else experts()

        @block.vector
        def _(dve):
            chain = Chain(dve, dve_chain)

            def norm(n):
                dve.wait_ge(squared, n + 1)
                dve.tensor_reduce(rstd[:], hT.rearrange("p k t -> p t k"), AX.X, ALU.add).then_inc(ssum_done, 1)
                dve.wait_ge(rms_done, n + 1)
                chain.step(dve.reciprocal(rstd[:], rstd[:]))
                chain.sync()
                for k in range(KD):
                    dve.tensor_tensor(hT[:, k, :], x[:, k, :], rstd[:], ALU.mult).then_inc(hn_done, 1)

            def modulation(l):
                dve.wait_ge(modT_done, ADA_N * (l + 1))
                if l:
                    dve.wait_ge(h_sample, KD * 2 * l)
                dve.tensor_tensor(mod[:], PS[:, 2, 0:96].rearrange("p (m c) -> p m c", c=2),
                                  bada[:, l, :].unsqueeze(2).to_broadcast([P, 48, 2]), ALU.add).then_inc(mod_done, 1)
                dve.wait_ge(mod_done, 3 * l + 1)
                for j in range(2):
                    dve.scalar_tensor_tensor(out=amod[:, j], in0=mod[:, 24 * j + 8:24 * j + 16, :], scalar=1.0,
                                             in1=gmix[:, l, j, :].unsqueeze(2).to_broadcast([P, KD, 2]),
                                             op0=ALU.add, op1=ALU.mult).then_inc(mod_done, 1)

            def add_gated(bank, m, gate, last_sem):
                for h, c0, c1, a, cond in ((0, 0, HALF, 0, 0), (1, 0, T_P - HALF, HALF, 0), (1, T_P - HALF, HALF, T_P, 1)):
                    w = x[:, m, a:a + c1 - c0]
                    ins = dve.scalar_tensor_tensor(out=w, in0=PS[:, bank + h, c0:c1], scalar=mod[:, gate + m, cond:cond + 1],
                                                   in1=w, op0=ALU.mult, op1=ALU.add)
                ins.then_inc(last_sem, 1)

            def rotate(dst, src, tab, t, n, heads):
                cos = tab[0:n, 0, t, :].unsqueeze(1).to_broadcast([n, heads, ROPE])
                sin = tab[0:n, 1, t, :].unsqueeze(1).to_broadcast([n, heads, ROPE])
                hr = ROPE // 2
                A, B = ropeA[0:n, 0:heads, :], ropeB[0:n, 0:heads, :]
                chain.step(dve.tensor_tensor(A, src, cos, ALU.mult))
                chain.step(dve.tensor_tensor(B[:, :, 0:hr], src[:, :, hr:ROPE], sin[:, :, 0:hr], ALU.mult))
                chain.step(dve.tensor_tensor(B[:, :, hr:ROPE], src[:, :, 0:hr], sin[:, :, hr:ROPE], ALU.mult))
                chain.sync()
                return dve.tensor_tensor(dst, A, B, ALU.add)

            def mixer(l):
                dve.wait_ge(tab_done, 6 * (l + 1))
                for t, (at, n) in enumerate(TILES):
                    b = t % 2
                    dve.wait_ge(z_stat, NT * l + t + 1)
                    chain.step(dve.reciprocal(rst[0:n, b, 0:3], rst[0:n, b, 0:3]))
                    chain.sync()
                    if t >= 2:
                        dve.wait_ge(lat_T, NT * l + t - 1)
                    chain.step(dve.tensor_scalar(tok[0:n, b, 0:Q_LORA], PS[0:n, b, 0:Q_LORA], rst[0:n, b, 0:1], None, ALU.mult))
                    dve.tensor_scalar(tok[0:n, b, Q_LORA:Q_LORA + KV_LORA], PS[0:n, b, Q_LORA:Q_LORA + KV_LORA], rst[0:n, b, 1:2],
                                      None, ALU.mult).then_inc(zn_done, 1)
                    chain.step(dve.tensor_scalar(ropeX[0:n, 0, :], PS[0:n, b, Q_LORA + KV_LORA:LAT], rst[0:n, b, 2:3], None, ALU.mult))
                    chain.sync()
                    kt = t if t < 4 else NKT - 1
                    if l == 1 and t == 0:
                        dve.wait_ge(out_sem, 16 * 6)
                        dve.wait_ge(krc_done, NKT)
                    rotate(kr[0:n, kt:kt + 1, :], ropeX[0:n, 0:1, :], ktab, t, n, 1).then_inc(kr_done, 1)
                for b in range(POOL_G):
                    if b == 0:
                        dve.wait_ge(u_copied, 3 * POOL_G * (l + 1))
                    w = 2 << b
                    dve.wait_ge(win_done, POOL_G * l + b + 1)
                    s = win[:, b % 2, :]
                    chain.step(dve.scalar_tensor_tensor(out=dT[:, b, 0:T_P], in0=s[:, HIST:S_AT], scalar=1.0 / w, in1=uE[:, b, HIST:S_AT],
                                                        op0=ALU.mult, op1=ALU.subtract))
                    dve.scalar_tensor_tensor(out=dT[:, b, T_P:T], in0=s[:, S_AT + HIST:EXT], scalar=1.0 / w, in1=uE[:, b, S_AT + HIST:EXT],
                                             op0=ALU.mult, op1=ALU.subtract).then_inc(d_done, 1)
                for j in range(QKT):
                    n = TILES[j][1] if j < NT else KTILES[j - NT][1]
                    b, b0 = j % 2, 2 * (j % 2)
                    dve.wait_ge(qk_sq, QKT * l + j + 1)
                    if j >= 2:
                        dve.wait_ge(qk_T, QKT * l + j - 1)
                    if j < NT:
                        heads = sq[0:n, b, :].rearrange("p (h c) -> p h c", h=NH)
                        chain.step(dve.tensor_reduce(stat[0:n, b, 0:8], heads[:, :, 0:NOPE], AX.X, ALU.add))
                        dve.tensor_reduce(stat[0:n, b, 8:16], heads[:, :, NOPE:QK], AX.X, ALU.add).then_inc(qk_sum, 1)
                    else:
                        heads = sq[0:n, b, 0:512].rearrange("p (h c) -> p h c", h=NH)
                        chain.step(dve.memset(stat[0:n, b, 8:16], 1.0))
                        dve.tensor_reduce(stat[0:n, b, 0:8], heads, AX.X, ALU.add).then_inc(qk_sum, 1)
                    dve.wait_ge(qk_rms, QKT * l + j + 1)
                    chain.step(dve.reciprocal(rst[0:n, b, :], rst[0:n, b, :]))
                    chain.sync()
                    rows = tok[0:n, b, :].rearrange("p (h c) -> p h c", h=NH)
                    if j < NT:
                        for g in range(2):
                            src = PS[0:n, b0 + g, 0:384].rearrange("p (h c) -> p h c", h=4)
                            r = rst[0:n, b, 4 * g:4 * g + 4].unsqueeze(2)
                            chain.step(dve.tensor_tensor(rows[:, 4 * g:4 * g + 4, 0:NOPE], src[:, :, 0:NOPE], r.to_broadcast([n, 4, NOPE]), ALU.mult))
                            r = rst[0:n, b, 8 + 4 * g:12 + 4 * g].unsqueeze(2)
                            chain.step(dve.tensor_tensor(ropeX[0:n, 4 * g:4 * g + 4, :], src[:, :, NOPE:QK], r.to_broadcast([n, 4, ROPE]), ALU.mult))
                        chain.sync()
                        rotate(rows[:, :, NOPE:QK], ropeX[0:n], qtab, j, n, NH).then_inc(qk_norm, 1)
                    else:
                        r = rst[0:n, b, 0:8].unsqueeze(2).to_broadcast([n, NH, NOPE])
                        dve.tensor_tensor(rows[:, :, 0:NOPE], PS[0:n, b0, :].rearrange("p (h c) -> p h c", h=NH), r,
                                          ALU.mult).then_inc(qk_norm, 1)
                U = len(UNITS)

                def normalise(u):
                    i, h = UNITS[u]
                    at, n = TILES[i]
                    nk = at + P if i < 4 else PAST + T_S
                    dve.wait_ge(exp_done, U * l + u + 1)
                    b = u % 2
                    chain.step(dve.reciprocal(rinv[0:n, b:b + 1], psumr[0:n, b:b + 1]))
                    chain.sync()
                    dve.tensor_scalar(prob[0:n, b, 0:nk], prob[0:n, b, 0:nk], rinv[0:n, b:b + 1], None, ALU.mult).then_inc(p_done, 1)

                def heads_done(i):
                    at, n = TILES[i]
                    dve.wait_ge(pv_done, U * l + NH * (i + 1))
                    dve.tensor_copy(hT[:, 0:4, at:at + n], PS[:, 4 + i % 2, :].rearrange("p (b t) -> p b t", b=4)[:, :, 0:n]).then_inc(o_copied, 1)

                for u in range(U + 1):
                    if u < U:
                        i, h = UNITS[u]
                        at, n = TILES[i]
                        nk = at + P if i < 4 else PAST + T_S
                        dve.wait_ge(s_done, U * l + u + 1)
                        if i < 4:
                            chain.step(dve.memset(PS[0:CHUNK, u % 2, nk - CHUNK:nk], NEG))
                            chain.sync()
                        dve.tensor_reduce(nmax[0:n, u % 2:u % 2 + 1], PS[0:n, u % 2, 0:nk], AX.X, ALU.max, negate=True).then_inc(max_done, 1)
                    if u >= 1:
                        normalise(u - 1)
                    if u >= NH + 3 and (u - 3) % NH == 0:
                        heads_done((u - 3) // NH - 1)
                heads_done(NT - 1)
                for m in range(KD):
                    dve.wait_ge(y_done, KD * l + m + 1)
                    add_gated(2 * (m % 4), m, 16, x_done)

            def route():
                dve.wait_ge(lg_done, 1)
                v = PS[:, 0, 0:NT * N_EXP].rearrange("p (t e) -> p t e", t=NT)
                brb = br[:].unsqueeze(1).to_broadcast([P, 4, N_EXP])
                chain.step(dve.tensor_tensor(logit[:, 0:4, :], v[:, 0:4, :], brb, ALU.add))
                chain.step(dve.tensor_tensor(logit[0:T_S, 4, :], v[0:T_S, 4, :], br[0:T_S, :], ALU.add))
                chain.sync()
                for t in range(NT):
                    chain.step(dve.max(top[:, t, :], logit[:, t, :]))
                chain.sync()
                for t in range(NT):
                    chain.step(dve.max_index(topi[:, t, :], top[:, t, :], logit[:, t, :]))
                chain.sync()
                chain.step(dve.tensor_copy(topf[:], topi[:]))
                dve.tensor_tensor(tw[:, :, 0:1], top[:, :, 1:2], top[:, :, 0:1], ALU.subtract).then_inc(tw_done, 1)
                chain.sync()
                each = lambda a: a.unsqueeze(1).to_broadcast([P, NT, N_EXP])
                for k in range(2):
                    chain.step(dve.tensor_tensor(oh[:, k], topf[:, :, k:k + 1].to_broadcast([P, NT, N_EXP]), each(iota8[:]), ALU.is_equal))
                chain.sync()
                chain.step(dve.tensor_tensor(picked[:], oh[:, 0], oh[:, 1], ALU.add))
                chain.sync()
                dve.memset(picked[T_S:P, NT - 1, :], 0.0).then_inc(picked_done, 1)
                dve.wait_ge(rank_done, 1)
                chain.step(dve.tensor_copy(rank[:].rearrange("p t e -> p (t e)"), PS[:, 1, 0:(NT + 1) * N_EXP]))
                chain.sync()
                cnt = rank[:, NT, :]
                for j in range(4):
                    chain.step(dve.tensor_scalar(over[:, j, :], cnt, float((j + 1) * P), None, ALU.is_gt))
                chain.sync()
                big = over[:, 2, :]
                chain.step(dve.memset(over[:, 4, 0:1], 0.0))
                for e in range(1, N_EXP):
                    chain.sync()
                    chain.step(dve.tensor_tensor(over[:, 4, e:e + 1], over[:, 4, e - 1:e], big[:, e - 1:e], ALU.add))
                chain.sync()
                chain.step(dve.tensor_tensor(over[:, 5, :], over[:, 4, :], econst[:, 2, :], ALU.add))
                chain.sync()
                chain.step(dve.tensor_scalar(over[:, 5, :], over[:, 5, :], float(GRP), None, ALU.mult))
                chain.step(dve.tensor_scalar(pos_e[:, 0], rank[:, 0:NT, :], float(GRP), None, ALU.is_ge))
                chain.step(dve.tensor_tensor(pos_e[:, 1], rank[:, 0:NT, :], each(econst[:, 1, :]), ALU.add))
                chain.sync()
                chain.step(dve.tensor_tensor(pos_e[:, 0], pos_e[:, 0], each(over[:, 5, :]), ALU.mult))
                chain.sync()
                chain.step(dve.tensor_tensor(pos_e[:, 0], pos_e[:, 0], pos_e[:, 1], ALU.add))
                chain.sync()
                for k in range(2):
                    chain.step(dve.tensor_tensor(oh[:, k], oh[:, k], pos_e[:, 0], ALU.mult))
                chain.sync()
                for k in range(2):
                    chain.step(dve.tensor_reduce(pos_f[:, k, :], oh[:, k], AX.X, ALU.add))
                chain.sync()
                dve.tensor_copy(pos[:], pos_f[:]).then_inc(pos_done, 1)
                chain.step(dve.scalar_tensor_tensor(out=tabf[:, 0:N_EXP], in0=over[:, 0, :], scalar=1.0, in1=over[:, 1, :], op0=ALU.add, op1=ALU.add))
                chain.step(dve.tensor_reduce(tabf[:, 12:13], big, AX.X, ALU.add))
                for j in range(MAX_OVER):
                    chain.sync()
                    chain.step(dve.scalar_tensor_tensor(out=pos_e[:, 1, 0, :], in0=over[:, 4, :], scalar=float(j), in1=big, op0=ALU.is_equal, op1=ALU.mult))
                    chain.sync()
                    chain.step(dve.tensor_tensor(pos_e[:, 1, 1, :], pos_e[:, 1, 0, :], econst[:, 0, :], ALU.mult))
                    chain.step(dve.scalar_tensor_tensor(out=pos_e[:, 1, 2, :], in0=over[:, 3, :], scalar=1.0, in1=pos_e[:, 1, 0, :], op0=ALU.add, op1=ALU.mult))
                    chain.sync()
                    chain.step(dve.tensor_reduce(tabf[:, 10 + j:11 + j], pos_e[:, 1, 1, :], AX.X, ALU.add))
                    chain.step(dve.tensor_reduce(tabf[:, N_EXP + j:N_EXP + j + 1], pos_e[:, 1, 2, :], AX.X, ALU.add))
                chain.sync()
                chain.step(dve.tensor_scalar(tabf[:, 13:14], tabf[:, 12:13], float(N_EXP), None, ALU.add))
                chain.sync()
                dve.tensor_copy(tab[:, 0:14], tabf[:, 0:14]).then_inc(tab_ready, 1)
                dve.wait_ge(top_done, 1)
                chain.step(dve.tensor_scalar(tw[:, :, 2:3], tw[:, :, 1:2], 1.0, None, ALU.add))
                chain.sync()
                chain.step(dve.reciprocal(tw[:, :, 3:4], tw[:, :, 2:3]))
                chain.sync()
                chain.step(dve.tensor_tensor(tw[:, :, 2:3], tw[:, :, 1:2], tw[:, :, 3:4], ALU.mult))
                dve.wait_ge(list_T, 1)
                dve.tensor_copy(slot_tok[:], PS[:, 1, 128:128 + N_LIST * GRP_T]).then_inc(list_done, 1)

            def split_unit(s, u):
                m, j = UNIT[u % UNITS_G]
                a, w = half(m, j)
                dve.wait_ge(hi_done, s * UNITS_G + u + 1)
                dve.tensor_tensor(w_lo[:, u % 4, 0:w], ring[:, m % MOE_SLOTS, a:a + w], w_hi[:, u % 4, 0:w].bitcast(F32),
                                  ALU.subtract).then_inc(lo_done, 1)

            def turned_group(i, t):
                dve.wait_ge(g_hi, i * GRP_T + t + 1)
                dve.tensor_tensor(hg_lo[:, :, t * P:(t + 1) * P], PS[:, 6:8, :].rearrange("p b (k t) -> p (b k) t", k=4),
                                  hg_hi[:, :, t * P:(t + 1) * P].bitcast(F32), ALU.subtract).then_inc(g_lo, 1)

            def group(i):
                n = dve.value_load(tab[0:1, bass.ds(i, 1)], min_val=1, max_val=GRP_T)

                def wide(op, s, *after):
                    with dve.If(n > 1):
                        for a in after:
                            dve.wait_ge(*a)
                        op(GRP_T).then_inc(s, 1)
                    with dve.Else():
                        for a in after:
                            dve.wait_ge(*a)
                        op(1).then_inc(s, 1)

                def turned_mid(u):
                    for f in TURN_MID.get(u, ()):
                        wide(lambda q: dve.tensor_tensor(mt_lo[:, f, 0:q * P], PS[:, 6 + f % 2, 0:q * P], mt_hi[:, f, 0:q * P].bitcast(F32),
                                                         ALU.subtract), m_lo, (m_hi, i * KF + f + 1))

                for u in range(UNITS_G):
                    if u in (17, 18):
                        turned_mid(u)
                    if 4 <= u <= 16 and u % 4 == 0:
                        c = u // 4 - 1
                        part = mg[:, :, c * W_GU:(c + 1) * W_GU]
                        wide(lambda q: dve.tensor_tensor(part[:, 0:q], part[:, 0:q], PS[:, 3:3 + q, 0:W_GU], ALU.mult),
                             gmid, (unit_done, i * UNITS_G + u), (gsilu, i * 4 + c + 1))
                    split_unit(i, u + 3)
                    if u < 17:
                        turned_mid(u)
                    if u in TURN_ROWS:
                        turned_group(i + 1, TURN_ROWS[u])

            def experts():
                for u in range(3):
                    split_unit(0, u)
                route()
                dve.memset(tabf[:, 14:16], 0.0).then_inc(y_copied, 4)
                dve.wait_ge(tab_ready, 1)
                for t in range(GRP_T):
                    turned_group(0, t)
                with dve.Fori(0, dve.value_load(tab[0:1, 13:14], min_val=N_EXP, max_val=N_EXP + MAX_OVER)) as i:
                    group(i)
                for t, (at, n) in enumerate(TILES):
                    b = t % 2
                    dve.wait_ge(back_in[b], 32 * (t // 2 + 1))
                    y1, y2 = rows4[0:n, 2 * b, :], rows4[0:n, 2 * b + 1, :]
                    chain.step(dve.tensor_scalar(y1, y1, tw[0:n, t, 3:4], None, ALU.mult))
                    chain.sync()
                    dve.scalar_tensor_tensor(out=y1, in0=y2, scalar=tw[0:n, t, 2:3], in1=y1, op0=ALU.mult, op1=ALU.add).then_inc(summed, 1)
                    if t:
                        add_back(t - 1)
                add_back(NT - 1)

            def add_back(t):
                at, n = TILES[t]
                dve.wait_ge(back_T, t + 1)
                cond = 0 if t < 4 else 1
                for k in range(KD):
                    w = x[:, k, at:at + n]
                    ins = dve.scalar_tensor_tensor(out=w, in0=PS[:, 2 * (t % 2) + k // 4, (k % 4) * P:(k % 4) * P + n],
                                                   scalar=mod[:, 40 + k, cond:cond + 1], in1=w, op0=ALU.mult, op1=ALU.add)
                ins.then_inc(added, 1)

            def ffn(l):
                g = layer_chunks(l)[2]
                for k in range(KD):
                    dve.wait_ge(h_split_hi, k + 1)
                    dve.tensor_tensor(h_lo[:, k, :], hT[:, k, :], h_hi[:, k, :].bitcast(F32), ALU.subtract).then_inc(h_split_lo, 1)
                with dve.Fori(0, N_DENSE_PARTS) as e:
                    def split(u):
                        c, a, w = dense_half(u)
                        dve.wait_ge(dw_split_hi, e * DENSE_UNITS + u + 1)
                        dve.tensor_tensor(dw_lo[:, u % 2, 0:w], ring[:, (g + c) % SLOTS, a:a + w], dw_hi[:, u % 2, 0:w].bitcast(F32),
                                          ALU.subtract).then_inc(dw_split_lo, 1)

                    split(0)
                    for u in range(DENSE_UNITS + 1):
                        turned = 2 <= u <= 2 * KF and u % 2 == 0
                        if turned:
                            c, b0 = u // 2 - 1, 4 * ((u // 2 - 1) % 2)
                            dve.wait_ge(silu_done, e * KF + c + 1)
                            dve.wait_ge(dense_unit, e * DENSE_UNITS + 2 * c + 4)
                            dve.tensor_tensor(mid[:, c % 2, :].rearrange("p (h t) -> p h t", h=2), sg[:, c % 2, :].rearrange("p (h t) -> p h t", h=2),
                                              PS[:, b0 + 2:b0 + 4, 0:HALF], ALU.mult).then_inc(mid_done, 1)
                        if u + 1 < DENSE_UNITS:
                            split(u + 1)
                        if turned:
                            dve.wait_ge(mid_split_hi, e * KF + c + 1)
                            dve.tensor_tensor(mid_lo[:, c, :], mid[:, c % 2, :], mid_hi[:, c, :].bitcast(F32), ALU.subtract).then_inc(mid_split_lo, 1)
                        if u > 2 * KF and u % 2 == 0:
                            m = (u - 2 * KF) // 2 - 1
                            dve.wait_ge(dense_unit, e * DENSE_UNITS + u + 2)
                            add_gated(2 * (m % 4), m, 40, acc_done)
                dve.memset(uE[:, :, 0:HIST], 0.0).then_inc(setup, 1)

            dve.memset(ones[:], 1.0).then_inc(acc_done, 1)
            dve.memset(logit[:], 0.0).then_inc(dense_unit, 2)
            dve.memset(uE[:, :, 0:HIST], 0.0)
            dve.memset(eps[:], EPS).then_inc(setup, 1)
            dve.wait_ge(const_in, 16 * CONSTS)
            dve.memset(g96[NOPE:QK, :, :], 1.0).then_inc(gains_set, 1)
            dve.wait_ge(gains_set, 1)
            dve.tensor_scalar(g96[:, :, 0], g96[:, :, 0], SCALE, None, ALU.mult).then_inc(gains_set, 1)
            for l in range(DEPTH):
                modulation(l)
                norm(2 * l)
                mixer(l)
                norm(2 * l + 1)
                ffn(l) if l == 0 else experts()

        @block.gpsimd
        def _(pool):
            chain = Chain(pool, pool_chain)

            def tables(l):
                if l:
                    pool.wait_ge(qk_norm, QKT)
                hr = ROPE // 2
                for j, tab in enumerate((qtab, ktab)):
                    for half, lo, hi in ((0, 0, ROPE), (1, 0, hr), (1, hr, ROPE)):
                        ga, gb = (lo, hi) if half == 0 else (hr - lo, hr - lo + hr)
                        pool.tensor_tensor(tab[:, half, :, lo:hi], cs[:, half, :, lo:hi],
                                           grow[:, l, j, ga:gb].unsqueeze(1).to_broadcast([P, NT, hi - lo]), ALU.mult).then_inc(tab_done, 1)

            def norm(n):
                l, which = n // 2, n % 2
                pool.wait_ge(mod_done, 3 * (l + 1))
                for k in range(KD):
                    pool.wait_ge(hn_done, KD * n + k + 1)
                    pool.tensor_scalar(hT[:, k, T_P:T], hT[:, k, T_P:T], amod[:, which, k, 1:2], mod[:, 24 * which + k, 1:2],
                                       ALU.mult, ALU.add).then_inc(h_sample, 1)

            def windows(l):
                pool.wait_ge(setup, l + 1)
                pool.wait_ge(past_in, 64 * (l + 1))
                for b in range(POOL_G):
                    pool.wait_ge(u_copied, 3 * (POOL_G * l + b + 1))
                    if b >= 1 or l:
                        pool.wait_ge(d_done, POOL_G * l + b)
                    src = uE[:, b, :]
                    for i in range(b + 1):
                        dst = win[:, (b + b - i) % 2, :]
                        step = 1 << i
                        lo = 2 * step - 1
                        chain.step(pool.tensor_tensor(dst[:, lo:EXT], src[:, lo:EXT], src[:, lo - step:EXT - step], ALU.add))
                        chain.sync()
                        src = dst
                    pool.tensor_tensor(src[:, HIST:HIST + 16], src[:, HIST:HIST + 16], ptab[:, b, :], ALU.mult).then_inc(win_done, 1)

            def rope_keys(l):
                for j in range(NKT):
                    n = KTILES[j][1]
                    jj = j + NT
                    pool.wait_ge(qk_T, QKT * l + jj - 1)
                    rows = tok[0:n, jj % 2, :].rearrange("p (h c) -> p h c", h=NH)
                    pool.tensor_copy(rows[:, :, NOPE:QK], kr[0:n, j:j + 1, :].to_broadcast([n, NH, ROPE])).then_inc(krc_done, 1)

            pool.memset(zeros[:], 0.0).then_inc(zero_set, 1)
            pool.memset(lists[:], 0.0).then_inc(zero_set, 1)
            pool.wait_ge(zero_set, 2)
            pool.dma_start(list_dst.rearrange("(g p) o -> g (p o)", p=P), lists[:]).then_inc(y_stored, 16)
            pool.wait_ge(const_in, 16 * CONSTS)
            for l in range(DEPTH):
                tables(l)
                norm(2 * l)
                windows(l)
                rope_keys(l)
                norm(2 * l + 1)
            pool.wait_ge(y_cleared, 16)
            pool.wait_ge(y_stored, 16)
            pool.wait_ge(pos_done, 1)
            for k in range(2):
                for t, (at, n) in enumerate(TILES):
                    pool.indirect_dma_start(list_dst, bass.IndirectOffsetOnAxis(pos[0:n, k, t:t + 1], 0), tok_id[0:n, t:t + 1],
                                            None).then_inc(scattered, 16)

            def gather(i):
                pool.tensor_copy(group_tok[:], slot_tok[:, bass.ds(i * GRP_T, GRP_T)]).then_inc(gtok_done, 1)
                pool.wait_ge(gtok_done, i + 1)
                n = None if isinstance(i, int) else pool.value_load(tab[0:1, bass.ds(i - 1, 1)], min_val=1, max_val=GRP_T)
                for t in range(GRP_T):
                    pool.indirect_dma_start(hg[:, t, :], None, row_dst, bass.IndirectOffsetOnAxis(group_tok[:, t:t + 1], 0)).then_inc(gathered, 16)
                return n

            pool.wait_ge(list_done, 1)
            for j in range(2):
                pool.wait_ge(rows_stored[j], 16 * len(range(j, NT, 2)))
            pool.wait_ge(rows_T, NT)
            gather(0)
            pool.wait_ge(tab_ready, 1)
            with pool.Fori(0, pool.value_load(tab[0:1, 13:14], min_val=N_EXP, max_val=N_EXP + MAX_OVER)) as i:
                pool.wait_ge(g_T, (i + 1) * GRP_T)
                n = gather(i + 1)
                dst = y_dst.rearrange("(g t p) n -> g p t n", t=GRP_T, p=P)[bass.ds(i, 1)].rearrange("a p t n -> (a p) t n")
                with pool.If(n > 1):
                    pool.wait_ge(y_copied, i * 4 + 8)
                    pool.dma_start(dst, yg).then_inc(y_stored, 16)
                with pool.Else():
                    pool.wait_ge(y_copied, i * 4 + 8)
                    pool.dma_start(dst[:, 0:1, :], yg[:, 0:1, :]).then_inc(y_stored, 16)
            groups = pool.value_load(tab[0:1, 13:14], min_val=N_EXP, max_val=N_EXP + MAX_OVER)
            pool.wait_ge(y_stored, (groups + 1) * 16)
            pool.value_load(tab[0:1, bass.ds(groups - 1, 1)], min_val=1, max_val=GRP_T)
            for t, (at, n) in enumerate(TILES):
                if t >= 2:
                    pool.wait_ge(back_T, t - 1)
                for k in range(2):
                    pool.indirect_dma_start(rows4[0:n, 2 * (t % 2) + k, :], None, y_dst, bass.IndirectOffsetOnAxis(pos[0:n, k, t:t + 1], 0)
                                            ).then_inc(back_in[t % 2], 16)


def constants():
    import numpy as np
    inv = (1.0 / (10000.0 ** (np.arange(0, ROPE, 2, dtype=np.float32) / np.float32(ROPE)))).astype(np.float32)
    pos = np.concatenate([np.arange(T_P), PAST + np.arange(T_S), np.zeros(NT * P - T)]).astype(np.float32)
    ang = (pos[:, None] * inv[None, :]).astype(np.float32).astype(np.float64)
    c, s = np.cos(ang), np.sin(ang)
    cs = np.stack([np.concatenate([c, c], 1), np.concatenate([-s, s], 1)]).astype(np.float32)
    cs = cs.reshape(2, NT, P, ROPE).transpose(2, 0, 1, 3)
    ptab = np.ones((P, POOL_G, 16), np.float32)
    for g in range(POOL_G):
        w = 2 << g
        ptab[:, g, :] = w / np.minimum(np.arange(16) + 1.0, w)
    iota8 = np.tile(np.arange(N_EXP, dtype=np.float32), (P, 1))
    p = np.arange(P)
    before = (p[:, None] < p[None, :]).astype(np.float32)
    e = np.arange(N_EXP)
    econst = np.tile(np.stack([e, GRP * e, N_EXP - 1 - e]).astype(np.float32), (P, 1, 1))
    tok_id = (np.arange(NT)[None, :] * P + p[:, None]).astype(np.float32)
    return {"before": before, "econst": econst, "tok_id": tok_id, "ident": np.eye(P, dtype=np.float32), "cs": np.ascontiguousarray(cs), "ptab": ptab, "iota8": iota8}


def kernel(**inp):
    import numpy as np
    import concourse.bacc as bacc
    from concourse.bass_utils import run_bass_kernel_spmd

    a = {k: np.asarray(v) for k, v in inp.items()}
    cols = lambda v: v.reshape(-1, v.shape[-1] // P, P)
    x = np.concatenate([a["x_prompt"][0], a["x_sample"][0]], 0)
    c = np.concatenate([a["c_prompt"], a["c_sample"]], 0)
    w_in = a["w_in"].reshape(DEPTH, KD, P, -1)
    w_lat = w_in[..., :LAT].transpose(0, 2, 1, 3)
    w_ukv = a["w_ukv"].reshape(DEPTH, KV_LORA, NH, NOPE + VD)
    w_ukv = np.concatenate([w_ukv[..., :NOPE].reshape(DEPTH, KV_LORA, -1), w_ukv[..., NOPE:].reshape(DEPTH, KV_LORA, -1)], -1)
    w_uq = a["w_uq"].reshape(DEPTH, 2, P, NH * QK).transpose(0, 2, 1, 3).reshape(DEPTH, P, -1)
    w_pool = a["w_pool"].transpose(0, 2, 1, 3).reshape(DEPTH, P, -1)

    def out_blocks(w, per):
        n, K, M = w.shape
        w = w.reshape(n, K // P, P, M // P // per, per, P)
        return w.transpose(0, 3, 2, 4, 1, 5).reshape(n, M // P // per, P, -1)

    def gate_up(g, u):
        g, u = out_blocks(g, 1), out_blocks(u, 1)
        return np.concatenate([g, u], -1)

    def expert_chunks(g, u, dn):
        gu = np.stack([g, u], 1).reshape(N_EXP, 2, KD, P, 4, W_GU).transpose(0, 4, 1, 3, 2, 5).reshape(N_EXP, 8, P, -1)
        dn = dn.reshape(N_EXP, KF, P, 4, W_DN).transpose(0, 3, 2, 1, 4).reshape(N_EXP, 4, P, -1)
        return np.concatenate([gu, dn], 1)

    def split(w):
        return w[0].reshape(D, N_DENSE_PARTS, F_EXP).transpose(1, 0, 2)

    arrays = {
        "x": x.T.reshape(KD, P, T).transpose(1, 0, 2),
        "c": c.T.reshape(KD, P, 2).transpose(1, 0, 2),
        "ada": a["w_ada"].reshape(DEPTH, KD, P, ADA_N, ADA_W).transpose(0, 3, 2, 1, 4).reshape(DEPTH, ADA_N, P, -1),
        "b_ada": cols(a["b_ada"]).transpose(2, 0, 1),
        "g_norm": np.stack([cols(a["g_mix"]), cols(a["g_ffn"])], 1).transpose(3, 0, 1, 2),
        "g_lat": np.concatenate([cols(a["g_q_lat"]), cols(a["g_kv_lat"])], 1).transpose(2, 0, 1),
        "g_nope": np.stack([a["g_qn_nope"], a["g_kn_nope"]], -1),
        "g_rope": np.stack([a["g_qn_rope"], a["g_kn_rope"]], 1),
        "pool_scale": cols(a["pool_scale"]).transpose(2, 0, 1),
        "w_router": a["w_router"][0].reshape(KD, P, N_EXP).transpose(1, 0, 2),
        "b_router": a["b_router"][0],
        "krope": a["cache_krope"].reshape(DEPTH, 2, P, ROPE),
        "ckv": a["cache_ckv"][:, 0].transpose(0, 2, 1),
        "hist": a["state_pool"][:, 0].reshape(DEPTH, HIST, POOL_G, P).transpose(0, 3, 2, 1),
        "w_t0": w_lat[:, :, 0:4].reshape(DEPTH, P, -1),
        "w_t1": np.concatenate([w_lat[:, :, 4:8].reshape(DEPTH, P, -1), w_pool], -1),
        "w_u": out_blocks(a["w_in"][..., LAT:], 2),
        "w_q": np.concatenate([w_uq, w_ukv], -1),
        "w_o": out_blocks(a["w_out"], 2),
        "w_gu": gate_up(split(a["w_ffn_gate"]), split(a["w_ffn_up"])),
        "w_dn": out_blocks(a["w_ffn_down"][0].reshape(N_DENSE_PARTS, F_EXP, D), 2),
        "e_w": expert_chunks(a["w_exp_gate"][0], a["w_exp_up"][0], a["w_exp_down"][0]),
    }
    arrays.update(constants())
    arrays = {f"in_{k}": np.ascontiguousarray(v) for k, v in arrays.items()}
    outs = {"y": (P, KD, T), "ckv": (DEPTH, P, T), "krope": (DEPTH, P, NT, ROPE), "pool": (DEPTH, P, POOL_G, 2, HIST)}

    nc = bacc.Bacc("TRN2", target_bir_lowering=False, num_devices=1)
    d = {k[3:]: nc.dram_tensor(k, v.shape, mybir.dt.from_np(v.dtype), kind="ExternalInput").ap() for k, v in arrays.items()}
    o = {k: nc.dram_tensor(f"out_{k}", s, F32, kind="ExternalOutput").ap() for k, s in outs.items()}
    build(nc, d, o)
    r = run_bass_kernel_spmd(nc, [arrays], core_ids=[0]).results[0]
    y = r["out_y"].transpose(1, 0, 2).reshape(D, T).T
    ckv = r["out_ckv"].transpose(0, 2, 1)
    kr = r["out_krope"].transpose(0, 2, 1, 3).reshape(DEPTH, NT * P, ROPE)
    pool = r["out_pool"].transpose(3, 0, 4, 2, 1).reshape(2, DEPTH, HIST, POOL_G * P)
    C = np.ascontiguousarray
    return (C(y[None, :T_P]), C(y[None, T_P:]), C(ckv[:, None, :T_P]), C(kr[:, None, :T_P]), C(pool[0][:, None]),
            C(ckv[:, None, T_P:]), C(kr[:, None, T_P:T]), C(pool[1][:, None]))
```
